# Optimizing a Trainium2 kernel written in Bass

```python
import math
import jax, jax.numpy as jnp
from jax import lax
import numpy as np

D_MODEL = 1024
BATCH = 1
SEQ = 256
DEPTH = 2

D_MIX = D_MODEL
D_MLSTM = D_MIX // 2
D_SB = D_MIX - D_MLSTM
H_MLSTM = 4
DH_MLSTM = D_MLSTM // H_MLSTM
H_SB = 8
DH_SB = D_SB // H_SB
CONV_K = 4
MLSTM_CHUNK = 64
SB_BLOCK = 128
P_IN = 4 * D_MLSTM + 2 * H_MLSTM + 3 * D_SB
D_FF_DENSE = 2752
N_EXPERTS = 8
TOP_K = 2
D_FF_EXPERT = 3584
N_DENSE_LAYERS = (DEPTH + 1) // 2
N_MOE_LAYERS = DEPTH // 2
EPS = 1e-6
M_INIT = -1e30

kernel_name = 'hybrid_mlstm_stickbreak_moe'

def _rmsnorm(x, g):
    xf = x.astype(jnp.float32)
    y = xf * lax.rsqrt(jnp.mean(xf * xf, axis=-1, keepdims=True) + EPS)
    return (y * g.astype(jnp.float32)).astype(x.dtype)

def _headwise_rmsnorm(x, g, n_heads):
    B, S, D = x.shape
    xf = x.astype(jnp.float32).reshape(B, S, n_heads, D // n_heads)
    y = xf * lax.rsqrt(jnp.mean(xf * xf, axis=-1, keepdims=True) + EPS)
    return y.reshape(B, S, D) * g.astype(jnp.float32)

def _to_heads(x, n_heads):
    B, S, D = x.shape
    return x.reshape(B, S, n_heads, D // n_heads).transpose(0, 2, 1, 3)

def _from_heads(x):
    B, H, S, dh = x.shape
    return x.transpose(0, 2, 1, 3).reshape(B, S, H * dh)

def _split_columns(proj):
    widths = (D_MLSTM, D_MLSTM, D_MLSTM, D_MLSTM, H_MLSTM, H_MLSTM, D_SB, D_SB, D_SB)
    out = []
    off = 0
    for w in widths:
        out.append(proj[..., off:off + w])
        off += w
    return out

def _causal_conv_silu(x, w, b):
    S = x.shape[1]
    xp = jnp.pad(x, ((0, 0), (CONV_K - 1, 0), (0, 0)))
    y = b
    for tap in range(CONV_K):
        y = y + xp[:, tap:tap + S, :] * w[tap]
    return jax.nn.silu(y)

def _mlstm_chunkwise(q, k, v, i_pre, f_pre):
    B, H, S, DH = q.shape
    L = MLSTM_CHUNK
    NC = S // L
    q = q.astype(jnp.float32)
    k = k.astype(jnp.float32) * (DH ** -0.5)
    v = v.astype(jnp.float32)
    log_i = i_pre.astype(jnp.float32)
    log_f = jax.nn.log_sigmoid(f_pre.astype(jnp.float32))

    def to_chunks(a):
        return jnp.moveaxis(a.reshape(B, H, NC, L, *a.shape[3:]), 2, 0)

    qc, kc, vc = to_chunks(q), to_chunks(k), to_chunks(v)
    ic, fc = to_chunks(log_i), to_chunks(log_f)
    causal = jnp.tril(jnp.ones((L, L), dtype=bool))

    def step(carry, inp):
        C, n, m = carry
        q_, k_, v_, i_, lf = inp
        b = jnp.cumsum(lf, axis=-1)
        d = b[..., :, None] - b[..., None, :] + i_[..., None, :]
        d = jnp.where(causal, d, -jnp.inf)
        inter = b + m[..., None]
        m_t = jnp.maximum(inter, jnp.max(d, axis=-1))
        w = jnp.exp(d - m_t[..., None])
        s = jnp.einsum('bhtd,bhsd->bhts', q_, k_) * w
        a_inter = jnp.exp(inter - m_t)
        num = a_inter[..., None] * jnp.einsum('bhtd,bhde->bhte', q_, C) + jnp.einsum('bhts,bhse->bhte', s, v_)
        den = a_inter * jnp.einsum('bhtd,bhd->bht', q_, n) + jnp.sum(s, axis=-1)
        h = num / jnp.maximum(jnp.abs(den), jnp.exp(-m_t))[..., None]
        b_last = b[..., -1]
        g = b_last[..., None] - b + i_
        m_new = jnp.maximum(b_last + m, jnp.max(g, axis=-1))
        decay = jnp.exp(b_last + m - m_new)
        wk = jnp.exp(g - m_new[..., None])[..., None] * k_
        C_new = decay[..., None, None] * C + jnp.einsum('bhsd,bhse->bhde', wk, v_)
        n_new = decay[..., None] * n + jnp.sum(wk, axis=2)
        return (C_new, n_new, m_new), h

    init = (jnp.zeros((B, H, DH, DH), jnp.float32),
            jnp.zeros((B, H, DH), jnp.float32),
            jnp.full((B, H), M_INIT, jnp.float32))
    _, hc = lax.scan(step, init, (qc, kc, vc, ic, fc))
    return jnp.moveaxis(hc, 0, 2).reshape(B, H, S, DH)

def _stick_breaking_attention(q, k, v):
    B, H, S, DH = q.shape
    scale = DH ** -0.5
    outs = []
    for blk in range(S // SB_BLOCK):
        t0 = blk * SB_BLOCK
        t1 = t0 + SB_BLOCK
        q_blk = q[:, :, t0:t1].astype(jnp.float32)
        k_blk = k[:, :, :t1].astype(jnp.float32)
        v_blk = v[:, :, :t1].astype(jnp.float32)
        z = jnp.einsum('bhtd,bhsd->bhts', q_blk, k_blk) * scale
        t_idx = t0 + jnp.arange(SB_BLOCK)[:, None]
        s_idx = jnp.arange(t1)[None, :]
        strict = s_idx < t_idx
        log_beta = jax.nn.log_sigmoid(z)
        log_rest = jnp.where(strict, jax.nn.log_sigmoid(-z), 0.0)
        rev = lax.cumsum(log_rest, axis=3, reverse=True)
        after = jnp.pad(rev[..., 1:], ((0, 0), (0, 0), (0, 0), (0, 1)))
        a = jnp.exp(jnp.where(strict, log_beta + after, -jnp.inf))
        outs.append(jnp.einsum('bhts,bhse->bhte', a, v_blk))
    return jnp.concatenate(outs, axis=2)

def _hybrid_mixer(h, w_in, b_igate, b_fgate, conv_w, conv_b, g_mlstm, g_sb, w_out):
    proj = h @ w_in
    q_m, k_m, v_m, o_m, i_pre, f_pre, q_s, k_s, v_s = _split_columns(proj)
    qk = _causal_conv_silu(jnp.concatenate([q_m, k_m], axis=-1), conv_w, conv_b)
    q_m, k_m = qk[..., :D_MLSTM], qk[..., D_MLSTM:]
    i_h = (i_pre + b_igate).transpose(0, 2, 1)
    f_h = (f_pre + b_fgate).transpose(0, 2, 1)
    h_m = _mlstm_chunkwise(_to_heads(q_m, H_MLSTM), _to_heads(k_m, H_MLSTM),
                           _to_heads(v_m, H_MLSTM), i_h, f_h)
    h_m = jax.nn.sigmoid(o_m.astype(jnp.float32)) * _headwise_rmsnorm(_from_heads(h_m), g_mlstm, H_MLSTM)
    h_s = _stick_breaking_attention(_to_heads(q_s, H_SB), _to_heads(k_s, H_SB), _to_heads(v_s, H_SB))
    h_s = _headwise_rmsnorm(_from_heads(h_s), g_sb, H_SB)
    mixed = jnp.concatenate([h_m, h_s], axis=-1).astype(h.dtype)
    return (mixed @ w_out).astype(h.dtype)

def _swiglu(h, w_gate, w_up, w_down):
    return (jax.nn.silu(h @ w_gate) * (h @ w_up)) @ w_down

def _moe_swiglu(h, w_router, w_gate, w_up, w_down):
    logits = (h @ w_router).astype(jnp.float32)
    top_val, top_idx = lax.top_k(logits, TOP_K)
    top_w = jax.nn.softmax(top_val, axis=-1)
    combine = jnp.sum(jax.nn.one_hot(top_idx, N_EXPERTS, dtype=jnp.float32) * top_w[..., None], axis=-2)
    combine = combine.astype(h.dtype)
    out = jnp.zeros_like(h)
    for e in range(N_EXPERTS):
        out = out + combine[..., e:e + 1] * _swiglu(h, w_gate[e], w_up[e], w_down[e])
    return out

def setup_inputs(seed: int = 0) -> dict:
    key = jax.random.key(seed)
    ks = jax.random.split(key, 20)
    f32 = jnp.float32
    nrm = lambda k, shape, fan_in: jax.random.normal(k, shape, f32) * (fan_in ** -0.5)
    return {
        'x': jax.random.normal(ks[0], (BATCH, SEQ, D_MODEL), f32),
        'norm_mix_g': 1.0 + 0.02 * jax.random.normal(ks[1], (DEPTH, D_MODEL), f32),
        'w_in': nrm(ks[2], (DEPTH, D_MODEL, P_IN), D_MODEL),
        'b_igate': 0.1 * jax.random.normal(ks[3], (DEPTH, H_MLSTM), f32),
        'b_fgate': 3.0 + 3.0 * jax.random.uniform(ks[4], (DEPTH, H_MLSTM), f32),
        'conv_w': nrm(ks[5], (DEPTH, CONV_K, 2 * D_MLSTM), CONV_K),
        'conv_b': 0.02 * jax.random.normal(ks[6], (DEPTH, 2 * D_MLSTM), f32),
        'g_mlstm': 1.0 + 0.02 * jax.random.normal(ks[7], (DEPTH, D_MLSTM), f32),
        'g_sb': 1.0 + 0.02 * jax.random.normal(ks[8], (DEPTH, D_SB), f32),
        'w_out': nrm(ks[9], (DEPTH, D_MIX, D_MODEL), D_MIX),
        'norm_ffn_g': 1.0 + 0.02 * jax.random.normal(ks[10], (DEPTH, D_MODEL), f32),
        'ffn_w_gate': nrm(ks[11], (N_DENSE_LAYERS, D_MODEL, D_FF_DENSE), D_MODEL),
        'ffn_w_up': nrm(ks[12], (N_DENSE_LAYERS, D_MODEL, D_FF_DENSE), D_MODEL),
        'ffn_w_down': nrm(ks[13], (N_DENSE_LAYERS, D_FF_DENSE, D_MODEL), D_FF_DENSE),
        'w_router': nrm(ks[14], (N_MOE_LAYERS, D_MODEL, N_EXPERTS), D_MODEL),
        'moe_w_gate': nrm(ks[15], (N_MOE_LAYERS, N_EXPERTS, D_MODEL, D_FF_EXPERT), D_MODEL),
        'moe_w_up': nrm(ks[16], (N_MOE_LAYERS, N_EXPERTS, D_MODEL, D_FF_EXPERT), D_MODEL),
        'moe_w_down': nrm(ks[17], (N_MOE_LAYERS, N_EXPERTS, D_FF_EXPERT, D_MODEL), D_FF_EXPERT),
        'norm_final_g': 1.0 + 0.02 * jax.random.normal(ks[18], (D_MODEL,), f32),
    }

def reference(x, norm_mix_g, w_in, b_igate, b_fgate, conv_w, conv_b, g_mlstm, g_sb, w_out,
              norm_ffn_g, ffn_w_gate, ffn_w_up, ffn_w_down, w_router, moe_w_gate, moe_w_up,
              moe_w_down, norm_final_g):
    h = x
    for layer in range(DEPTH):
        y = _rmsnorm(h, norm_mix_g[layer])
        h = h + _hybrid_mixer(y, w_in[layer], b_igate[layer], b_fgate[layer], conv_w[layer],
                              conv_b[layer], g_mlstm[layer], g_sb[layer], w_out[layer])
        y = _rmsnorm(h, norm_ffn_g[layer])
        j = layer // 2
        if layer % 2 == 0:
            h = h + _swiglu(y, ffn_w_gate[j], ffn_w_up[j], ffn_w_down[j])
        else:
            h = h + _moe_swiglu(y, w_router[j], moe_w_gate[j], moe_w_up[j], moe_w_down[j])
    return _rmsnorm(h, norm_final_g)


_drawn_inputs = setup_inputs


def setup_inputs(seed=0):
    import zlib

    import numpy as np

    out = dict(_drawn_inputs(seed))
    spreads = {}
    factors = {'b_igate': 38.205,
     'conv_b': 3.439,
     'g_mlstm': 2.902,
     'norm_final_g': 8.381,
     'g_sb': 3.972,
     'norm_ffn_g': 3.289}
    for name, (base, spread) in spreads.items():
        noise = np.random.default_rng([zlib.crc32(name.encode()), seed]).standard_normal(out[name].shape)
        drawn = base * np.exp(spread * noise) if base else spread * noise
        out[name] = __import__('jax').numpy.asarray(drawn.astype(out[name].dtype))
    for name, factor in factors.items():
        out[name] = (out[name] * factor).astype(out[name].dtype)
    return out
```

```python
from contextlib import ExitStack

import concourse.bass as bass
from concourse import mybir

F32 = mybir.dt.float32
F32R = mybir.dt.float32r
BF16 = mybir.dt.bfloat16
I32 = mybir.dt.int32
ALU = mybir.AluOpType
ACT = mybir.ActivationFunctionType
AX = mybir.AxisListType

P = 128
TT = 2
D = 1024
KC = D // P
DEPTH = 2
HM, DHM = 4, 128
HS, DHS = 8, 64
CONV_K = 4
DM = HM * DHM
GATES = 4 * DM
SBC = GATES + 2 * HM
F_DENSE = 2752
F_EXPERT = 3584
E = 8
FB = 512
NEG = -1e30
EPS = 1e-6

NRAW = 6
NSPLIT = 3
PIECE = 2048
QS, KS, VS, QM, KM, VM, OM = range(7)
BLOCKS = 7
FIRST_COLUMN = [SBC, SBC + 512, SBC + 1024, 0, DM, 2 * DM, 3 * DM]
OUT_PIECES = (2, 3, 0, 1)
MIX_PIECES = 2 * BLOCKS + 4
DENSE_FULL = F_DENSE // FB
TAIL = F_DENSE - DENSE_FULL * FB
FFN_PIECES = 6 * DENSE_FULL + 3
EB = F_EXPERT // FB
JOB_PIECES = 6 * EB
MIX_BASE = [0, MIX_PIECES + FFN_PIECES]
FFN_BASE = MIX_PIECES
MOE_BASE = 2 * MIX_PIECES + FFN_PIECES
EXTRA = 3
JOBS = E + EXTRA


def gate_piece(f, half):
    return half if f == 0 else 4 + 6 * (f - 1) + half


def down_piece(f, half, blocks):
    return 8 + 6 * f + half if f < blocks - 1 else 6 * blocks - 2 + half


class Loop:

    def __init__(self):
        self.reg, self.per = None, {}

    def at(self, kind, value):
        return value if self.reg is None else self.reg * self.per[kind] + value


def trunk(nc, x, norm_mix_g, w_in, b_igate, b_fgate, conv_w, conv_b, g_mlstm, g_sb, w_out,
          norm_ffn_g, ffn_w_gate, ffn_w_up, ffn_w_down, w_router, moe_w_gate, moe_w_up,
          moe_w_down, norm_final_g, out):
    with ExitStack() as ctx:
        def sb(name, shape, dt=F32):
            return ctx.enter_context(nc.sbuf_tensor(name, shape, dt))

        def sem(name):
            return ctx.enter_context(nc.semaphore(name))

        raw = sb("raw", [P, NRAW, PIECE])
        whi = sb("whi", [P, NSPLIT, PIECE], F32R)
        wlo = sb("wlo", [P, NSPLIT, PIECE], F32R)
        h = sb("h", [P, TT, D])
        y = sb("y", [P, TT, D])
        gains = sb("gains", [P, 2, D])
        xT_hi = sb("xT_hi", [P, KC, TT * P], F32R)
        xT_lo = sb("xT_lo", [P, KC, TT * P], F32R)
        hid_hi = sb("hid_hi", [P, 2, 1024], F32R)
        hid_lo = sb("hid_lo", [P, 2, 1024], F32R)
        scatT = sb("scatT", [P, TT, P], F32R)
        scratch = sb("scratch", [P, 3616])
        qkc = sb("qkc", [P, 8, 256])
        vm = sb("vm", [P, TT, HM, DHM + 2])
        om = sb("om", [P, TT, DM])
        qsT = sb("qsT", [P, 4, 256])
        ksT = sb("ksT", [P, 4, 256])
        vs = sb("vs", [P, TT, 512])
        neg_max = sb("neg_max", [HM, TT * P])
        ident = sb("ident", [P, P])
        ident_b = sb("ident_b", [P, P], BF16)
        zero_b = sb("zero_b", [P, P], BF16)
        mask_m = sb("mask_m", [P, P], BF16)
        mask_s = sb("mask_s", [P, P], BF16)
        tri_neg = sb("tri_neg", [P, P])
        neg1 = sb("neg1", [P, P])
        tri = sb("tri", [P, P])
        ones = sb("ones", [P, 256])
        iota_i = sb("iota_i", [P, P], I32)
        iota = sb("iota", [P, P])
        iota_e = sb("iota_e", [P, E])
        desc_e = sb("desc_e", [P, E])
        sel = sb("sel", [HM, HM, P])
        eps = sb("eps", [P, 1])
        convp = sb("convp", [P, KC, DEPTH * (CONV_K + 1)])
        wif = sb("wif", [P, DEPTH, 64])
        wif_hi = sb("wif_hi", [P, DEPTH, 64], F32R)
        wif_lo = sb("wif_lo", [P, DEPTH, 64], F32R)
        wr = sb("wr", [P, KC, E])
        gbias = sb("gbias", [HM, DEPTH, 2])
        ssq = sb("ssq", [P, 2])
        rms = sb("rms", [P, 2])
        lnv = sb("lnv", [P, 2])
        rstd = sb("rstd", [P, 2])
        gate_t = sb("gate_t", [P, TT, 8])
        acol = sb("acol", [P, TT, HM])
        emcol = sb("emcol", [P, TT, HM])
        den = sb("den", [P, TT, HM])
        msc = sb("msc", [P, 6, TT * HM])
        ssc = sb("ssc", [P, 4, TT * HS])
        rt = sb("rt", [P, 16, TT, E])
        job_pos = sb("job_pos", [P, TT, JOBS])
        job_w = sb("job_w", [P, TT, JOBS])
        ovf = sb("ovf", [P, 8, E])
        table = sb("table", [P, 4])
        table_i = sb("table_i", [1, 4], I32)

        ps = ctx.enter_context(nc.psum_tensor("ps", [P, 8, 512], F32))

        qkp = scratch[:, 0:2080].rearrange("p (c t) -> p c t", c=8)
        convrow = scratch[0:10, 2080:3104]
        zt = scratch[:, 2080:2848].rearrange("p (b t) -> p b t", b=2)
        softp = scratch[:, 2848:3616].rearrange("p (b t) -> p b t", b=2)
        aT = zt
        decay = scratch[:, 0:768].rearrange("p (b t) -> p b t", b=2)
        pT = scratch[:, 768:1536].rearrange("p (b t) -> p b t", b=2)
        squares = scratch[:, 2080:3104].rearrange("p (a t) -> p a t", a=2)
        unused = [scratch[:, c:c + 256].rearrange("p (t d) -> p t d", t=TT)
                  for c in (1536, 1792, 3104, 3360)]
        silu = scratch[:, 0:1024]
        prod = scratch[:, 1024:2048]
        slots = scratch[:, 2048:2304].rearrange("p (a t) -> p a t", a=2)
        o_hi, o_lo = hid_hi[:, :, 512:], hid_lo[:, :, 512:]
        rows = [y[0:HM, r // 2, 256 * (r % 2):256 * (r % 2) + 256] for r in range(4)]
        rows += [om[0:HM, r // 2, 256 * (r % 2):256 * (r % 2) + 256] for r in range(3)]
        rows += [neg_max[:]]
        xT_f = qkc

        arrived = [sem(f"arrived{i}") for i in range(NRAW)]
        hi_ready = sem("hi_ready")
        lo_ready = sem("lo_ready")
        piece_used = sem("piece_used")
        x_in = sem("x_in")
        small_in = sem("small_in")
        first_gain_in = sem("first_gain_in")
        gain_in = [sem("gain_in0"), sem("gain_in1")]
        consts = sem("consts")
        vm_ones = sem("vm_ones")
        wif_in = sem("wif_in")
        pool_step = sem("pool_step")
        conv_ps = sem("conv_ps")
        convp_ready = sem("convp_ready")
        wif_hi_ready = sem("wif_hi_ready")
        wif_ready = sem("wif_ready")
        h_ready = sem("h_ready")
        ssq_ready = sem("ssq_ready")
        rms_ready = sem("rms_ready")
        rstd_ready = sem("rstd_ready")
        msum = sem("msum")
        mrms = sem("mrms")
        ssum = sem("ssum")
        srms = sem("srms")
        act_step = sem("act_step")
        dve_step = sem("dve_step")
        m_rows = sem("m_rows")
        y_ready = sem("y_ready")
        xT_ps = sem("xT_ps")
        xT_hi_ready = sem("xT_hi_ready")
        xT_ready = sem("xT_ready")
        proj_out = sem("proj_out")
        conv_done = sem("conv_done")
        silu_done = sem("silu_done")
        gate_ps = sem("gate_ps")
        gate_sb = sem("gate_sb")
        grow_ps = sem("grow_ps")
        fabs = sem("fabs")
        flog = sem("flog")
        grows = sem("grows")
        gcol_ps = sem("gcol_ps")
        gcol = sem("gcol")
        head_ps = sem("head_ps")
        decay_ready = sem("decay_ready")
        pT_ready = sem("pT_ready")
        num_ps = sem("num_ps")
        num_out = sem("num_out")
        z_ps = sem("z_ps")
        lnz_ready = sem("lnz_ready")
        softp_ready = sem("softp_ready")
        sum_ps = sem("sum_ps")
        aT_ready = sem("aT_ready")
        av_ps = sem("av_ps")
        av_out = sem("av_out")
        sil_ready = sem("sil_ready")
        prod_ready = sem("prod_ready")
        hid_hi_ready = sem("hid_hi_ready")
        hid_ready = sem("hid_ready")
        route_ps = sem("route_ps")
        rexp_in = sem("rexp_in")
        rexp = sem("rexp")
        chosen = sem("chosen")
        count_ps = sem("count_ps")
        table_ready = sem("table_ready")
        slots_ready = sem("slots_ready")
        scatT_ps = sem("scatT_ps")
        scatT_ready = sem("scatT_ready")
        xg_ps = sem("xg_ps")
        xg_hi_ready = sem("xg_hi_ready")
        xg_ready = sem("xg_ready")
        e_sil = sem("e_sil")
        e_prod = sem("e_prod")
        e_hidT = sem("e_hidT")
        e_hid_hi = sem("e_hid_hi")
        e_hid = sem("e_hid")
        o_hi_ready = sem("o_hi_ready")
        o_ready = sem("o_ready")
        scat_ps = sem("scat_ps")
        job_done = sem("job_done")
        stored = sem("stored")

        block = ctx.enter_context(nc.Block())
        PER_JOB = {"piece": JOB_PIECES, "block": EB, "job": 1, "tile": TT}

        @block.sync
        def _(sp):
            loop = Loop()

            def load(i, parts):
                if loop.reg is not None or i >= NRAW:
                    sp.wait_ge(lo_ready, loop.at("piece", i - NRAW + 1))
                for place, src in parts:
                    sp.dma_start(place, src).then_inc(arrived[i % NRAW], 16)

            def cols(i, w, half, c0, n=FB):
                v = raw[:, i % NRAW, :].rearrange("p (k n) -> p k n", k=4)
                rows_ = w[half * 512:(half + 1) * 512, bass.ds(c0, n)]
                load(i, [(v, rows_.rearrange("(k p) n -> p k n", p=P))])

            def two_rows(i, w, r0):
                v = raw[:, i % NRAW, :].rearrange("p (k n) -> p k n", k=2)
                load(i, [(v, w[bass.ds(r0, 256), :].rearrange("(k p) n -> p k n", p=P))])

            def mixer(l):
                n = MIX_BASE[l]
                for b in range(BLOCKS):
                    for half in range(2):
                        cols(n + 2 * b + half, w_in[l], half, FIRST_COLUMN[b])
                for i in range(4):
                    two_rows(n + 2 * BLOCKS + i, w_out[l], 256 * OUT_PIECES[i])

            sp.dma_start(h[:], x[0].rearrange("(t p) d -> p t d", p=P)).then_inc(x_in, 16)
            mixer(0)
            n = FFN_BASE
            wg, wu, wd = ffn_w_gate[0], ffn_w_up[0], ffn_w_down[0]
            for half in range(2):
                cols(n + half, wg, half, 0)
            for half in range(2):
                cols(n + 2 + half, wu, half, 0)
            with sp.Fori(0, DENSE_FULL - 1) as r:
                loop.reg, loop.per = r, {"piece": 6}
                for half in range(2):
                    cols(n + 4 + half, wg, half, (r + 1) * FB)
                for half in range(2):
                    cols(n + 6 + half, wu, half, (r + 1) * FB)
                for half in range(2):
                    two_rows(n + 8 + half, wd, r * FB + 256 * half)
            loop.reg = None
            n += 6 * DENSE_FULL - 2
            c0 = DENSE_FULL * FB
            for w in (wg, wu):
                v = raw[:, n % NRAW, 0:KC * TAIL].rearrange("p (k n) -> p k n", k=KC)
                load(n, [(v, w[:, c0:].rearrange("(k p) n -> p k n", p=P))])
                n += 1
            for half in range(2):
                two_rows(n, wd, c0 - FB + 256 * half)
                n += 1
            v = raw[:, n % NRAW, :].rearrange("p (k n) -> p k n", k=2)
            load(n, [(v[:, 0], wd[c0:c0 + P, :]), (v[:, 1], wd[F_DENSE - P:, :])])
            mixer(1)

            def job(e):
                n = MOE_BASE

                def expert(w):
                    return w[0, bass.ds(e, 1)].rearrange("e r c -> (e r) c")

                for f in range(EB):
                    for w, o in ((moe_w_gate, 0), (moe_w_up, 2)):
                        for half in range(2):
                            cols(n + gate_piece(f, half) + o, expert(w), half, f * FB)
                    if f:
                        for half in range(2):
                            two_rows(n + down_piece(f - 1, half, EB), expert(moe_w_down),
                                     (f - 1) * FB + 256 * half)
                for half in range(2):
                    two_rows(n + down_piece(EB - 1, half, EB), expert(moe_w_down),
                             (EB - 1) * FB + 256 * half)

            with sp.Fori(0, E) as j:
                loop.reg, loop.per = j, {"piece": JOB_PIECES}
                job(j)
            sp.wait_ge(table_ready, 1)
            jobs = sp.value_load(table_i[0:1, 3:4], min_val=E, max_val=JOBS)
            with sp.Fori(E, JOBS) as j:
                loop.reg = j
                with sp.If(j < jobs):
                    e = sp.value_load(table_i[0:1, bass.ds(j - E, 1)], min_val=0, max_val=E - 1)
                    job(e)
            loop.reg = None
            sp.wait_ge(y_ready, 18)
            sp.dma_start(out[0].rearrange("(t p) d -> p t d", p=P), y[:]).then_inc(stored, 16)
            sp.wait_ge(stored, 16)

        @block.gpsimd
        def _(pool):
            steps = [0]

            def step(ins):
                steps[0] += 1
                ins.then_inc(pool_step, 1)

            for t, v in ((ident, 0.0), (ident_b, 0.0), (mask_m, 0.0), (mask_s, 0.0),
                         (tri_neg, -1.0), (tri, 1.0), (sel, 0.0)):
                step(pool.memset(t[:], v))
            pool.iota(iota_i[:], [[1, P]], base=0, channel_multiplier=0).then_inc(pool_step, 1)
            pool.memset(neg1[:], -1.0).then_inc(consts, 1)
            pool.memset(ones[:], 1.0).then_inc(consts, 1)
            pool.memset(eps[:], EPS).then_inc(consts, 1)
            pool.memset(zero_b[:], 0.0).then_inc(consts, 1)
            pool.wait_ge(pool_step, steps[0] + 1)
            for t in (ident, ident_b):
                pool.affine_select(out=t[:], in_=t[:], compare_op=ALU.not_equal, fill=1.0, base=0,
                                   pattern=[[-1, P]], channel_multiplier=1).then_inc(consts, 1)
            for t, base in ((mask_m, 0), (mask_s, -1)):
                pool.affine_select(out=t[:], in_=t[:], compare_op=ALU.is_ge, fill=NEG, base=base,
                                   pattern=[[1, P]], channel_multiplier=-1).then_inc(consts, 1)
            pool.affine_select(out=tri_neg[:], in_=tri_neg[:], compare_op=ALU.is_ge, fill=0.0,
                               base=0, pattern=[[-1, P]], channel_multiplier=1).then_inc(consts, 1)
            pool.affine_select(out=tri[:], in_=tri[:], compare_op=ALU.is_ge, fill=0.0,
                               base=-1, pattern=[[1, P]], channel_multiplier=-1).then_inc(consts, 1)
            pool.affine_select(out=sel[:], in_=sel[:], compare_op=ALU.not_equal, fill=1.0, base=0,
                               pattern=[[-1, HM], [0, P]], channel_multiplier=1).then_inc(consts, 1)
            pool.tensor_copy(iota[:], iota_i[:]).then_inc(consts, 1)
            pool.wait_ge(consts, 12)
            pool.tensor_copy(iota_e[:], iota[:, 0:E]).then_inc(consts, 1)
            pool.tensor_scalar(desc_e[:], iota[:, 0:E], -1.0, float(E), ALU.mult, ALU.add
                               ).then_inc(consts, 1)
            pool.memset(vm[:], 1.0).then_inc(vm_ones, 1)
            for l in range(DEPTH):
                r0 = l * (CONV_K + 1)
                pool.dma_start(convrow[r0:r0 + CONV_K, :], conv_w[l]).then_inc(small_in, 16)
                pool.dma_start(convrow[r0 + CONV_K:r0 + CONV_K + 1, :],
                               conv_b[l:l + 1, :]).then_inc(small_in, 16)
                for i, b in enumerate((b_igate, b_fgate)):
                    pool.dma_start(gbias[:, l, i:i + 1],
                                   b[l].rearrange("(h o) -> h o", o=1)).then_inc(small_in, 16)
            pool.dma_start(wr[:], w_router[0].rearrange("(k p) e -> p k e", p=P)).then_inc(small_in, 16)

            def gain(u, *parts):
                if u >= 2:
                    pool.wait_ge(y_ready, 2 * (0, 0, 1, 3, 4, 5, 7)[u])
                c = 0
                for g in parts:
                    n = g.shape[-1]
                    pool.dma_start(gains[:, u % 2, c:c + n],
                                   g.rearrange("(a n) -> a n", a=1).to_broadcast([P, n])
                                   ).then_inc(gain_in[u % 2], 16)
                    c += n

            gain(1, g_mlstm[0], g_sb[0])
            gain(2, norm_ffn_g[0])
            gain(3, norm_mix_g[1])
            gain(4, g_mlstm[1], g_sb[1])
            gain(5, norm_ffn_g[1])
            gain(6, norm_final_g)
        CONSTS = 14
        SMALL = 16 * 9

        @block.scalar
        def _(act):
            loop = Loop()
            done = [0]
            steps = [0]

            def own(ins):
                steps[0] += 1
                ins.then_inc(act_step, 1)
                act.wait_ge(act_step, steps[0])

            def split(i):
                act.wait_ge(arrived[i % NRAW], arrival(i, loop))
                if loop.reg is not None or i >= NSPLIT:
                    act.wait_ge(piece_used, loop.at("piece", i - NSPLIT + 1))
                act.activation(whi[:, i % NSPLIT, :], raw[:, i % NRAW, :], ACT.Copy
                               ).then_inc(hi_ready, 1)

            def split_upto(i):
                while done[0] <= i:
                    split(done[0])
                    done[0] += 1

            def tables(name):
                act.preload_act_table_set(name)

            def norm_stats(u):
                tables("sqrt_and_others")
                if u == 4:
                    act.wait_ge(job_done, jobs + 1)
                for t in range(TT):
                    if u == 0:
                        act.wait_ge(x_in, 16)
                    elif u < 4:
                        act.wait_ge(h_ready, 2 * (u - 1) + t + 1)
                    act.activation(y[:, t, :], h[:, t, :], ACT.Square, scale=D ** -0.5,
                                   accum_out=ssq[:, t:t + 1]).then_inc(ssq_ready, 1)
                    act.wait_ge(ssq_ready, TT * u + t + 1)
                    act.activation(rms[:, t:t + 1], ssq[:, t:t + 1], ACT.Sqrt, bias=eps[:]
                                   ).then_inc(rms_ready, 1)

            def xT_copy(q):
                for t in range(TT):
                    act.wait_ge(xT_ps, 2 * q + t + 1)
                    s = slice(t * P, (t + 1) * P)
                    act.activation(xT_hi[:, :, s], xT_bank(t), ACT.Copy).then_inc(xT_hi_ready, 1)

            def xT_copy_half(q, half, bank):
                for t in range(TT):
                    act.wait_ge(xT_ps, 2 * q + t + 1)
                    act.activation(xT_hi[:, 4 * half:4 * half + 4, t * P:(t + 1) * P],
                                   ps[:, bank + t, :].rearrange("p (c t) -> p c t", t=P), ACT.Copy
                                   ).then_inc(xT_hi_ready, 1)

            def xT_bank(t):
                return ps[:, 2 * t:2 * t + 2, :].rearrange("p b (c t) -> p (b c) t", t=P)

            def mixer(l, q):
                n = MIX_BASE[l]
                split_upto(n + 2)
                norm_stats(2 * l)
                if l == 0:
                    act.wait_ge(wif_in, 32)
                    act.activation(wif_hi[:], wif[:], ACT.Copy).then_inc(wif_hi_ready, 1)
                xT_copy(q)

                act.wait_ge(gate_ps, l + 1)
                act.activation(gate_t[:], ps[:, 6, 0:16].rearrange("p (t c) -> p t c", t=TT),
                               ACT.Copy).then_inc(gate_sb, 1)

                def evacuate(b):
                    act.wait_ge(piece_used, n + 2 * b + 2)
                    bank = ps[:, 2 * (b % 2):2 * (b % 2) + 2, :]
                    if b in (QM, KM):
                        g = b - QM
                        ins = act.activation(qkp[:, 4 * g:4 * g + 4, 3:259],
                                             bank.rearrange("p b (c t) -> p (b c) t", t=256), ACT.Copy)
                    elif b == VM:
                        act.wait_ge(vm_ones, 1)
                        for t in range(TT):
                            ins = act.activation(vm[:, t, :, 0:DHM],
                                                 bank[:, t, :].rearrange("p (h d) -> p h d", h=HM),
                                                 ACT.Copy)
                            if t == 0:
                                ins.then_inc(act_step, 1)
                                steps[0] += 1
                    elif b == OM:
                        ins = act.activation(om[:], bank, ACT.Exp, scale=-1.0)
                    elif b == VS:
                        ins = act.activation(vs[:], bank, ACT.Copy)
                    else:
                        dst = qsT if b == QS else ksT
                        ins = act.activation(dst[:], bank.rearrange("p b (c t) -> p (b c) t", t=256),
                                             ACT.Copy, scale=DHS ** -0.5 if b == QS else 1.0)
                    ins.then_inc(proj_out, 1)

                def gate_rows():
                    act.wait_ge(fabs, l + 1)
                    own(act.activation(rows[3], rows[2], ACT.Exp, scale=-1.0))
                    act.activation(rows[4], rows[3], ACT.Ln, bias=ones[0:HM, 0:1]
                                   ).then_inc(flog, 1)

                def gate_columns():
                    act.wait_ge(gcol_ps, l + 1)
                    v = ps[:, 6, 64:80].rearrange("p (m t h) -> p m t h", m=2, t=TT)
                    act.activation(acol[:], v[:, 0], ACT.Copy).then_inc(act_step, 1)
                    act.activation(emcol[:], v[:, 1], ACT.Exp, scale=-1.0).then_inc(act_step, 1)
                    steps[0] += 2
                    act.wait_ge(act_step, steps[0])
                    act.activation(lnv[:, 0:1], eps[:], ACT.Copy).then_inc(gcol, 1)

                def decays(hd):
                    k = 4 * l + hd
                    act.wait_ge(head_ps, 2 * k + 1)
                    if hd >= 2:
                        act.wait_ge(pT_ready, k - 1)
                    for j, s in ((0, slice(0, 256)), (1, slice(256, 384))):
                        act.activation(decay[:, hd % 2, s], ps[:, 2, s], ACT.Exp,
                                       bias=acol[:, j, hd:hd + 1]).then_inc(decay_ready, 1)

                def numerators(hd):
                    act.wait_ge(num_ps, 4 * l + hd + 1)
                    v = ps[:, hd % 2, 0:260].rearrange("p (t d) -> p t d", t=TT)
                    act.activation(y[:, :, hd * P:(hd + 1) * P], v[:, :, 0:P], ACT.Copy
                                   ).then_inc(num_out, 1)
                    act.activation(den[:, :, hd:hd + 1], v[:, :, P:P + 1], ACT.Copy
                                   ).then_inc(num_out, 1)
                    for t in range(TT):
                        c = HM * t + hd
                        act.activation(unused[hd][:, t], v[:, t, 0:P], ACT.Square,
                                       accum_out=msc[:, 5, c:c + 1]).then_inc(num_out, 1)

                def soft(p):
                    z = ps[:, 4:6, 0:384]
                    act.wait_ge(z_ps, 4 * l + p + 1)
                    own(act.activation(zt[:], z, ACT.Abs))
                    steps[0] += 1
                    act.activation(zt[:], zt[:], ACT.Exp, scale=-1.0).then_inc(act_step, 1)
                    tables("natural_log")
                    act.wait_ge(act_step, steps[0])
                    act.activation(zt[:], zt[:], ACT.Ln, bias=ones[:, 0:1]).then_inc(lnz_ready, 1)
                    tables("exp_and_others")

                def pair_weights(p):
                    act.wait_ge(sum_ps, 4 * l + p + 1)
                    act.activation(aT[:], ps[:, 4:6, 0:384], ACT.Exp).then_inc(aT_ready, 1)

                def pair_rows(p):
                    act.wait_ge(av_ps, 4 * l + p + 1)
                    c = 512 + p * P
                    act.activation(y[:, :, c:c + P], ps[:, 7, 0:256].rearrange(
                        "p (t d) -> p t d", t=TT), ACT.Copy).then_inc(av_out, 1)

                for b in range(BLOCKS):
                    for half in range(2):
                        i = 2 * b + half
                        split_upto(n + i + 3)
                        if half == 1:
                            evacuate(b)
                        if i == 0 and l == 0:
                            act.wait_ge(conv_ps, 1)
                            act.activation(convp[:], ps[:, 6, 128:208].rearrange(
                                "p (c k) -> p c k", c=KC), ACT.Copy).then_inc(convp_ready, 1)
                        if i == 1:
                            gate_rows()
                            tables("exp_and_others")
                        if i == 4:
                            gate_columns()
                        if i % 2 == 0 and 6 <= i <= 12:
                            pair_rows(i // 2 - 3)
                        if i % 2 == 0 and 4 <= i <= 10:
                            soft(i // 2 - 2)
                        if i % 2 == 1 and 5 <= i <= 11:
                            pair_weights(i // 2 - 2)
                        if i == 11:
                            tables("silu_and_others")
                            for g in range(2):
                                act.wait_ge(conv_done, 2 * l + g + 1)
                                act.activation(qkc[:, 4 * g:4 * g + 4, :], qkc[:, 4 * g:4 * g + 4, :],
                                               ACT.Silu).then_inc(silu_done, 1)
                            tables("exp_and_others")
                        if i == 12:
                            decays(0)
                            tables("sqrt_and_others")
                            act.wait_ge(ssum, l + 1)
                            act.activation(ssc[:, 1, :], ssc[:, 0, :], ACT.Sqrt, scale=1.0 / DHS,
                                           bias=eps[:]).then_inc(srms, 1)
                            tables("exp_and_others")

                decays(1)
                numerators(0)
                xT_copy_half(q + 1, 1, 4)
                decays(2)
                numerators(1)
                decays(3)
                tables("sqrt_and_others")
                numerators(2)
                numerators(3)
                split_upto(n + 2 * BLOCKS + 3)
                act.wait_ge(msum, l + 1)
                act.activation(msc[:, 3, :], msc[:, 2, :], ACT.Sqrt, scale=1.0 / DHM, bias=eps[:]
                               ).then_inc(mrms, 1)
                split_upto(n + 2 * BLOCKS + 4)
                xT_copy_half(q + 2, 0, 0)
                for i in (2, 3):
                    split_upto(n + 2 * BLOCKS + i + 3)

            act.dma_start(gains[:, 0, :], norm_mix_g[0].rearrange("(a n) -> a n", a=1)
                          .to_broadcast([P, D])).then_inc(first_gain_in, 16)
            for l in range(DEPTH):
                act.dma_start(wif[:, l, :].rearrange("p (k c) -> p k c", k=KC),
                              w_in[l][:, GATES:SBC].rearrange("(k p) c -> p k c", p=P)
                              ).then_inc(wif_in, 16)
            act.wait_ge(consts, CONSTS)
            mixer(0, 0)

            norm_stats(1)
            tables("silu_and_others")
            xT_copy(3)

            def hidden(f, width=1024):
                act.wait_ge(piece_used, loop.at("piece", FFN_BASE + gate_piece(f, 0) + 4)
                            if f < DENSE_FULL else FFN_BASE + 6 * DENSE_FULL)
                act.activation(silu[:, 0:width], ps[:, 0:width // 512, :], ACT.Silu
                               ).then_inc(sil_ready, 1)
                act.wait_ge(prod_ready, loop.at("block", f + 1))
                act.activation(hid_hi[:, f % 2, 0:width], prod[:, 0:width], ACT.Copy
                               ).then_inc(hid_hi_ready, 1)

            n = FFN_BASE
            for i in range(4):
                split_upto(n + i + 3)
            hidden(0)
            with act.Fori(0, (DENSE_FULL - 1) // 2) as r:
                loop.reg, loop.per = r, {"piece": 12, "block": 2}
                for f in (1, 2):
                    for i in range(6):
                        split(n + 4 + 6 * (f - 1) + i + 3)
                        if i == 3:
                            hidden(f)
            loop.reg = None
            done[0] = n + 4 + 24 + 3
            n += 6 * DENSE_FULL - 2
            for i in range(5):
                split_upto(n + i + 3)
                if i == 1:
                    hidden(DENSE_FULL, 512)
            mixer(1, 4)

            norm_stats(3)
            for t in range(TT):
                act.wait_ge(xT_ps, 2 * 7 + t + 1)
                act.activation(xT_f[:, :, t * P:(t + 1) * P], xT_bank(t), ACT.Copy
                               ).then_inc(xT_hi_ready, 1)
            act.wait_ge(rexp_in, 1)
            act.activation(rt[:, 10, :, 0:1], rt[:, 9, :, 0:1], ACT.Exp).then_inc(rexp, 1)

            tables("silu_and_others")
            act.wait_ge(table_ready, 1)
            jobs = act.value_load(table_i[0:1, 3:4], min_val=E, max_val=JOBS)
            n = MOE_BASE

            def gathered(o):
                act.wait_ge(xg_ps, loop.at("job", 1 + o))
                act.activation(xT_hi[:, :, 0:P],
                               ps[:, 2:4, :].rearrange("p b (c t) -> p b c t", t=P),
                               ACT.Copy).then_inc(xg_hi_ready, 1)

            def scatter_matrix(o):
                act.wait_ge(scatT_ps, loop.at("job", 1 + o))
                act.activation(scatT[:], ps[:, 6, 0:256].rearrange("p (t c) -> p t c", t=TT),
                               ACT.Copy).then_inc(scatT_ready, 1)

            def e_silu(i, f, o=0):
                act.wait_ge(piece_used, loop.at("piece", n + i + 1))
                act.activation(silu[:, 0:512], ps[:, 2 * (f % 2), :], ACT.Silu).then_inc(e_sil, 1)

            def hid_high(f):
                act.wait_ge(e_hidT, loop.at("block", f + 1))
                if f >= 2:
                    act.wait_ge(piece_used, loop.at("piece", n + down_piece(f - 2, 1, EB) + 1))
                act.activation(hid_hi[:, f % 2, 0:512], ps[:, 4 + f % 2, :], ACT.Copy
                               ).then_inc(e_hid_hi, 1)

            def rest_of_job(then_next):
                for i in range(4, JOB_PIECES + (4 if then_next else 0)):
                    if then_next or i + NSPLIT < JOB_PIECES:
                        split(n + i + NSPLIT)
                    for f in range(1, EB):
                        if i == gate_piece(f, 1):
                            hid_high(f - 1)
                        if i == gate_piece(f, 1) + 2:
                            e_silu(i, f)
                    if i == JOB_PIECES - 3:
                        hid_high(EB - 1)
                        if then_next:
                            gathered(1)
                    if i == JOB_PIECES - 1:
                        act.wait_ge(piece_used, loop.at("piece", n + JOB_PIECES))
                        act.activation(o_hi, ps[:, 6:8, :], ACT.Copy).then_inc(o_hi_ready, 1)
                    if i == JOB_PIECES + 1:
                        scatter_matrix(1)
                    if i == JOB_PIECES + 3:
                        e_silu(i, 0)

            def start_of_job():
                gathered(0)
                scatter_matrix(0)
                for i in range(4):
                    split(n + i + NSPLIT)
                e_silu(3, 0)

            start_of_job()
            with act.Fori(0, E - 1) as j:
                loop.reg, loop.per = j, PER_JOB
                rest_of_job(then_next=True)
            loop.reg = E - 1
            rest_of_job(then_next=False)
            with act.Fori(E, JOBS) as j:
                with act.If(j < jobs):
                    loop.reg = j
                    for i in range(NSPLIT):
                        split(n + i)
                    start_of_job()
                    rest_of_job(then_next=False)
            loop.reg = None
            norm_stats(4)

        @block.vector
        def _(dve):
            loop = Loop()
            done = [0]
            steps = [0]

            def own(ins):
                steps[0] += 1
                ins.then_inc(dve_step, 1)
                dve.wait_ge(dve_step, steps[0])

            def split(i):
                dve.wait_ge(hi_ready, loop.at("piece", i + 1))
                dve.tensor_tensor(wlo[:, i % NSPLIT, :], raw[:, i % NRAW, :],
                                  whi[:, i % NSPLIT, :].bitcast(F32), ALU.subtract).then_inc(lo_ready, 1)

            def split_upto(i):
                while done[0] <= i:
                    split(done[0])
                    done[0] += 1

            gains_in = [0, 32, 16, 48, 48, 64, 64]

            def norm_rows(k, u):
                if u == 0:
                    dve.wait_ge(first_gain_in, 16)
                else:
                    dve.wait_ge(gain_in[u % 2], gains_in[u])
                for t in range(TT):
                    dve.wait_ge(rms_ready, TT * k + t + 1)
                    dve.reciprocal(rstd[:, t:t + 1], rms[:, t:t + 1]).then_inc(rstd_ready, 1)
                    dve.wait_ge(rstd_ready, TT * k + t + 1)
                    dve.scalar_tensor_tensor(y[:, t, :], h[:, t, :], rstd[:, t:t + 1],
                                             gains[:, u % 2, :], ALU.mult, ALU.mult
                                             ).then_inc(y_ready, 1)

            def xT_rest(q):
                for t in range(TT):
                    dve.wait_ge(xT_hi_ready, 2 * q + t + 1)
                    s = slice(t * P, (t + 1) * P)
                    bank = ps[:, 2 * t:2 * t + 2, :].rearrange("p b (c t) -> p (b c) t", t=P)
                    dve.tensor_tensor(xT_lo[:, :, s], bank, xT_hi[:, :, s].bitcast(F32), ALU.subtract
                                      ).then_inc(xT_ready, 1)

            def xT_rest_half(q, half, bank):
                for t in range(TT):
                    dve.wait_ge(xT_hi_ready, 2 * q + t + 1)
                    v = slice(4 * half, 4 * half + 4), slice(t * P, (t + 1) * P)
                    dve.tensor_tensor(xT_lo[:, v[0], v[1]],
                                      ps[:, bank + t, :].rearrange("p (c t) -> p c t", t=P),
                                      xT_hi[:, v[0], v[1]].bitcast(F32), ALU.subtract
                                      ).then_inc(xT_ready, 1)

            def mixer(l, q):
                n = MIX_BASE[l]
                split_upto(n + 2)
                norm_rows(2 * l, 3 * l)
                if l == 0:
                    dve.wait_ge(wif_hi_ready, 1)
                    dve.tensor_tensor(wif_lo[:], wif[:], wif_hi[:].bitcast(F32), ALU.subtract
                                      ).then_inc(wif_ready, 1)
                dve.memset(qkp[:, :, 0:3], 0.0).then_inc(dve_step, 1)
                steps[0] += 1
                xT_rest(q)

                def convolve(g):
                    dve.wait_ge(proj_out, 7 * l + QM + g + 1)
                    for tap in range(CONV_K):
                        for c in range(4 * g, 4 * g + 4):
                            w = convp[:, c, 5 * l + tap:5 * l + tap + 1]
                            src = qkp[:, c, tap:tap + 256]
                            if tap == 0:
                                ins = dve.tensor_scalar(qkc[:, c, :], src, w,
                                                        convp[:, c, 5 * l + 4:5 * l + 5],
                                                        ALU.mult, ALU.add)
                            else:
                                dve.wait_ge(dve_step, steps[0] - 3)
                                ins = dve.scalar_tensor_tensor(qkc[:, c, :], src, w, qkc[:, c, :],
                                                               ALU.mult, ALU.add)
                            if (tap, c % 4) == (CONV_K - 1, 3):
                                dve.wait_ge(dve_step, steps[0])
                                ins.then_inc(conv_done, 1)
                            else:
                                ins.then_inc(dve_step, 1)
                                steps[0] += 1

                def gate_rows():
                    dve.wait_ge(grow_ps, l + 1)
                    dve.wait_ge(small_in, SMALL)
                    for i in range(2):
                        own(dve.tensor_scalar(rows[i], ps[0:HM, 7, 256 * i:256 * i + 256],
                                              gbias[:, l, i:i + 1], None, ALU.add))
                    dve.scalar_tensor_tensor(rows[2], rows[1], -1.0, rows[1], ALU.mult, ALU.max
                                             ).then_inc(fabs, 1)
                    dve.wait_ge(flog, l + 1)
                    own(dve.scalar_tensor_tensor(rows[5], rows[1], 0.0, rows[4],
                                                 ALU.min, ALU.subtract))
                    own(dve.tensor_tensor_scan(rows[2], ones[0:HM, :], rows[5], 0.0,
                                               ALU.mult, ALU.add))
                    own(dve.tensor_tensor(rows[6], rows[0], rows[2], ALU.subtract))
                    own(dve.tensor_tensor_scan(rows[3], rows[6], rows[6], NEG,
                                               ALU.max, ALU.max))
                    own(dve.tensor_tensor(rows[5], rows[3], rows[2], ALU.add))
                    dve.tensor_scalar(rows[7], rows[3], -1.0, None, ALU.mult
                                      ).then_inc(grows, 1)

                def weights(hd):
                    k = 4 * l + hd
                    dve.wait_ge(head_ps, 2 * k + 2)
                    dve.wait_ge(decay_ready, 2 * k + 2)
                    if hd >= 2:
                        dve.wait_ge(num_ps, k - 1)
                    dve.scalar_tensor_tensor(pT[:, hd % 2, :], ps[:, 3, 0:384], DHM ** -0.5,
                                             decay[:, hd % 2, :], ALU.mult, ALU.mult
                                             ).then_inc(pT_ready, 1)

                def soft(p):
                    k = 4 * l + p
                    dve.wait_ge(lnz_ready, k + 1)
                    if p:
                        dve.wait_ge(sum_ps, k)
                    dve.scalar_tensor_tensor(softp[:], ps[:, 4:6, 0:384], 0.0, zt[:], ALU.max,
                                             ALU.add).then_inc(softp_ready, 1)

                u = 3 * l + 1
                g = gains[:, u % 2, :]

                def stick_norm():
                    dve.wait_ge(av_out, 4 * (l + 1))
                    own(dve.tensor_tensor(squares[:], y[:, :, 512:], y[:, :, 512:], ALU.mult))
                    for t in range(TT):
                        ins = dve.tensor_reduce(ssc[:, 0, HS * t:HS * t + HS],
                                                squares[:, t, :].rearrange("p (h d) -> p h d", h=HS),
                                                AX.X, ALU.add)
                        if t == 0:
                            own(ins)
                    ins.then_inc(ssum, 1)
                    dve.wait_ge(srms, l + 1)
                    own(dve.reciprocal(ssc[:, 2, :], ssc[:, 1, :]))
                    dve.wait_ge(gain_in[u % 2], gains_in[u])
                    for t in range(TT):
                        ys = y[:, t, 512:].rearrange("p (h d) -> p h d", h=HS)
                        own(dve.tensor_tensor(ys, ys, spread(ssc[:, 2, HS * t:HS * t + HS], DHS),
                                              ALU.mult))
                        dve.tensor_tensor(y[:, t, 512:], y[:, t, 512:], g[:, 512:], ALU.mult
                                          ).then_inc(y_ready, 1)

                for b in range(BLOCKS):
                    for half in range(2):
                        i = 2 * b + half
                        split_upto(n + i + 3)
                        if i == 1:
                            gate_rows()
                        if i == 8:
                            dve.wait_ge(convp_ready, 1)
                            convolve(0)
                        if i == 10:
                            convolve(1)
                        if i % 2 == 0 and 4 <= i <= 10:
                            soft(i // 2 - 2)
                        if i == 12:
                            weights(0)
                            stick_norm()

                weights(1)
                dve.wait_ge(proj_out, 7 * (l + 1))
                own(dve.tensor_scalar(om[:], om[:], 1.0, None, ALU.add))
                xT_rest_half(q + 1, 1, 4)
                weights(2)
                own(dve.reciprocal(om[:], om[:]))
                weights(3)
                for t in range(TT):
                    own(dve.tensor_tensor(om[:, t, :], om[:, t, :], g[:, 0:512], ALU.mult))
                dve.wait_ge(num_out, 16 * (l + 1))
                dve.wait_ge(gcol, l + 1)
                flat = den[:].rearrange("p t h -> p (t h)")
                own(dve.scalar_tensor_tensor(msc[:, 0, :], flat, -1.0, flat, ALU.mult, ALU.max))
                own(dve.tensor_tensor(msc[:, 0, :], msc[:, 0, :],
                                      emcol[:].rearrange("p t h -> p (t h)"), ALU.max))
                own(dve.reciprocal(msc[:, 1, :], msc[:, 0, :]))
                own(dve.tensor_tensor(msc[:, 2, :], msc[:, 5, :], msc[:, 1, :], ALU.mult))
                dve.tensor_tensor(msc[:, 2, :], msc[:, 2, :], msc[:, 1, :], ALU.mult).then_inc(msum, 1)
                dve.wait_ge(mrms, l + 1)
                own(dve.reciprocal(msc[:, 4, :], msc[:, 3, :]))
                own(dve.tensor_tensor(msc[:, 4, :], msc[:, 4, :], msc[:, 1, :], ALU.mult))
                for t in range(TT):
                    for hd in range(HM):
                        s = slice(hd * P, (hd + 1) * P)
                        ins = dve.scalar_tensor_tensor(y[:, t, s], y[:, t, s],
                                                       msc[:, 4, HM * t + hd:HM * t + hd + 1],
                                                       om[:, t, s], ALU.mult, ALU.mult)
                        ins.then_inc(m_rows, 1)
                    dve.wait_ge(m_rows, HM * (TT * l + t + 1))
                    dve.memset(lnv[:, t:t + 1], 0.0).then_inc(y_ready, 1)
                split_upto(n + 2 * BLOCKS + 3)
                xT_rest_half(q + 2, 0, 0)
                for i in (1, 2, 3):
                    split_upto(n + 2 * BLOCKS + i + 3)
                add_rows(n + MIX_PIECES)

            def spread(v, n):
                return v.rearrange("p (h o) -> p h o", o=1).to_broadcast([P, v.shape[1], n])

            def add_rows(used):
                dve.wait_ge(piece_used, used)
                for t in range(TT):
                    dve.tensor_tensor(h[:, t, :].rearrange("p (b c) -> p b c", b=2),
                                      h[:, t, :].rearrange("p (b c) -> p b c", b=2),
                                      ps[:, 4 + 2 * t:6 + 2 * t, :], ALU.add).then_inc(h_ready, 1)

            dve.wait_ge(consts, CONSTS)
            mixer(0, 0)

            norm_rows(1, 2)
            xT_rest(3)

            def hidden(f, width=1024):
                dve.wait_ge(sil_ready, loop.at("block", f + 1))
                dve.tensor_tensor(prod[:, 0:width], silu[:, 0:width],
                                  ps[:, 2:2 + width // 512, :].rearrange("p b c -> p (b c)"), ALU.mult
                                  ).then_inc(prod_ready, 1)
                dve.wait_ge(hid_hi_ready, loop.at("block", f + 1))
                dve.tensor_tensor(hid_lo[:, f % 2, 0:width], prod[:, 0:width],
                                  hid_hi[:, f % 2, 0:width].bitcast(F32), ALU.subtract
                                  ).then_inc(hid_ready, 1)

            n = FFN_BASE
            for i in range(4):
                split_upto(n + i + 3)
            hidden(0)
            with dve.Fori(0, (DENSE_FULL - 1) // 2) as r:
                loop.reg, loop.per = r, {"piece": 12, "block": 2}
                for f in (1, 2):
                    for i in range(6):
                        split(n + 4 + 6 * (f - 1) + i + 3)
                        if i == 3:
                            hidden(f)
            loop.reg = None
            done[0] = n + 4 + 24 + 3
            n += 6 * DENSE_FULL - 2
            for i in range(5):
                split_upto(n + i + 3)
                if i == 1:
                    hidden(DENSE_FULL, 512)
            add_rows(n + 5)
            mixer(1, 4)

            norm_rows(3, 5)
            dve.wait_ge(route_ps, 1)
            own(dve.tensor_copy(rt[:, 0], ps[:, 4, 0:16].rearrange("p (t e) -> p t e", t=TT)))
            for c in range(2):
                logit, best, hit, pick = 5 * c, 5 * c + 1, 5 * c + 2, 5 * c + 3
                if c:
                    own(dve.scalar_tensor_tensor(rt[:, 5], rt[:, 3], -3e38, rt[:, 0],
                                                 ALU.mult, ALU.add))
                    own(dve.tensor_scalar(rt[:, 5], rt[:, 5], -3e38, None, ALU.max))
                own(dve.tensor_reduce(rt[:, best, :, 0:1], rt[:, logit], AX.X, ALU.max))
                for t in range(TT):
                    own(dve.scalar_tensor_tensor(rt[:, hit, t], rt[:, logit, t], rt[:, best, t, 0:1],
                                                 desc_e[:], ALU.is_equal, ALU.mult))
                own(dve.tensor_reduce(rt[:, best, :, 1:2], rt[:, hit], AX.X, ALU.max))
                for t in range(TT):
                    own(dve.tensor_scalar(rt[:, pick, t], desc_e[:], rt[:, best, t, 1:2], None,
                                          ALU.is_equal))
            own(dve.tensor_tensor(rt[:, 4], rt[:, 3], rt[:, 8], ALU.add))
            dve.tensor_tensor(rt[:, 9, :, 0:1], rt[:, 6, :, 0:1], rt[:, 1, :, 0:1], ALU.subtract
                              ).then_inc(rexp_in, 1)
            own(dve.tensor_copy(rt[:, 15], rt[:, 4]))
            dve.wait_ge(rexp_in, 1)
            dve.tensor_copy(rt[:, 14], rt[:, 4]).then_inc(chosen, 1)
            dve.wait_ge(rexp, 1)
            own(dve.tensor_scalar(rt[:, 11, :, 0:1], rt[:, 10, :, 0:1], 1.0, None, ALU.add))
            own(dve.reciprocal(rt[:, 11, :, 0:1], rt[:, 11, :, 0:1]))
            own(dve.tensor_tensor(rt[:, 11, :, 1:2], rt[:, 11, :, 0:1], rt[:, 10, :, 0:1], ALU.mult))
            for t in range(TT):
                own(dve.tensor_scalar(rt[:, 12, t], rt[:, 3, t], rt[:, 11, t, 0:1], None, ALU.mult))
                own(dve.scalar_tensor_tensor(job_w[:, t, 0:E], rt[:, 8, t], rt[:, 11, t, 1:2],
                                             rt[:, 12, t], ALU.mult, ALU.add))
            dve.wait_ge(count_ps, 1)
            pos = ps[:, 5, 0:16].rearrange("p (t e) -> p t e", t=TT)
            own(dve.tensor_scalar(rt[:, 13], pos, 1.0, None, ALU.add))
            own(dve.tensor_tensor(rt[:, 13], rt[:, 13], rt[:, 4], ALU.mult))
            own(dve.tensor_scalar(job_pos[:, :, 0:E], rt[:, 13], -1.0, None, ALU.add))
            own(dve.tensor_scalar(ovf[:, 0], ps[:, 5, 16:24], float(P), None, ALU.is_gt))
            own(dve.tensor_tensor_scan(ovf[:, 1], ones[:, 0:E], ovf[:, 0], 0.0, ALU.mult, ALU.add))
            own(dve.tensor_scalar(table[:, 3:4], ovf[:, 1, E - 1:E], float(E), None, ALU.add))
            for r in range(EXTRA):
                own(dve.scalar_tensor_tensor(ovf[:, 2], ovf[:, 1], float(r + 1), ovf[:, 0],
                                             ALU.is_equal, ALU.mult))
                own(dve.tensor_tensor(ovf[:, 3], ovf[:, 2], iota_e[:], ALU.mult))
                own(dve.tensor_reduce(table[:, r:r + 1], ovf[:, 3], AX.X, ALU.add))
                for t in range(TT):
                    own(dve.scalar_tensor_tensor(ovf[:, 4], job_pos[:, t, 0:E], -float(P), ovf[:, 2],
                                                 ALU.add, ALU.mult))
                    own(dve.tensor_reduce(job_pos[:, t, E + r:E + r + 1], ovf[:, 4], AX.X, ALU.add))
                    own(dve.tensor_tensor(ovf[:, 5], job_w[:, t, 0:E], ovf[:, 2], ALU.mult))
                    own(dve.tensor_reduce(job_w[:, t, E + r:E + r + 1], ovf[:, 5], AX.X, ALU.add))
            dve.tensor_copy(table_i[:], table[0:1, :]).then_inc(table_ready, 1)
            dve.memset(ssq[:], 0.0).then_inc(job_done, 1)

            dve.wait_ge(table_ready, 1)
            jobs = dve.value_load(table_i[0:1, 3:4], min_val=E, max_val=JOBS)
            n = MOE_BASE

            def one_hot(o):
                if loop.reg is not None:
                    dve.wait_ge(scatT_ps, loop.at("job", o))
                for t in range(TT):
                    at = job_pos[:, t, bass.ds(loop.reg + o, 1)] if loop.reg is not None \
                        else job_pos[:, t, 0:1]
                    dve.tensor_scalar(slots[:, t, :], iota[:], at, None, ALU.is_equal
                                      ).then_inc(slots_ready, 1)

            def gathered(o):
                dve.wait_ge(xg_hi_ready, loop.at("job", 1 + o))
                dve.tensor_tensor(xT_lo[:, :, 0:P],
                                  ps[:, 2:4, :].rearrange("p b (c t) -> p b c t", t=P),
                                  xT_hi[:, :, 0:P].rearrange("p (b c) t -> p b c t", b=2).bitcast(F32),
                                  ALU.subtract).then_inc(xg_ready, 1)

            def hid_low(f):
                dve.wait_ge(e_hid_hi, loop.at("block", f + 1))
                dve.tensor_tensor(hid_lo[:, f % 2, 0:512], ps[:, 4 + f % 2, :],
                                  hid_hi[:, f % 2, 0:512].bitcast(F32), ALU.subtract
                                  ).then_inc(e_hid, 1)

            def e_product(f, o=0):
                dve.wait_ge(e_sil, loop.at("block", f + 1 + EB * o))
                dve.tensor_tensor(prod[:, 0:512], silu[:, 0:512], ps[:, 2 * (f % 2) + 1, :],
                                  ALU.mult).then_inc(e_prod, 1)

            def add_job():
                dve.wait_ge(scat_ps, loop.at("job", 1))
                dve.wait_ge(job_done, loop.at("job", 1))
                for t in range(TT):
                    ht = h[:, t, :].rearrange("p (b c) -> p b c", b=2)
                    w = job_w[:, t, bass.ds(loop.reg, 1)]
                    ins = dve.scalar_tensor_tensor(ht, ps[:, 2:4, :] if t == 0 else ps[:, 4:6, :],
                                                   w, ht, ALU.mult, ALU.add)
                    if t == 0:
                        ins.then_inc(dve_step, 1)
                ins.then_inc(job_done, 1)

            def rest_of_job(then_next):
                for i in range(4, JOB_PIECES + (4 if then_next else 0)):
                    if then_next or i + NSPLIT < JOB_PIECES:
                        split(n + i + NSPLIT)
                    for f in range(1, EB):
                        if i == gate_piece(f, 1):
                            hid_low(f - 1)
                        if i == gate_piece(f, 1) + 2:
                            e_product(f)
                    if i == JOB_PIECES // 2 and then_next:
                        one_hot(1)
                    if i == JOB_PIECES - 3:
                        hid_low(EB - 1)
                        if then_next:
                            gathered(1)
                    if i == JOB_PIECES - 1:
                        dve.wait_ge(o_hi_ready, loop.at("job", 1))
                        dve.tensor_tensor(o_lo, ps[:, 6:8, :], o_hi.bitcast(F32), ALU.subtract
                                          ).then_inc(o_ready, 1)
                        if not then_next:
                            add_job()
                    if i == JOB_PIECES + 1:
                        add_job()
                    if i == JOB_PIECES + 3:
                        e_product(0, 1)

            def start_of_job():
                gathered(0)
                for i in range(4):
                    split(n + i + NSPLIT)
                e_product(0)

            one_hot(0)
            start_of_job()
            with dve.Fori(0, E - 1) as j:
                loop.reg, loop.per = j, PER_JOB
                rest_of_job(then_next=True)
            loop.reg = E - 1
            rest_of_job(then_next=False)
            with dve.Fori(E, JOBS) as j:
                with dve.If(j < jobs):
                    loop.reg = j
                    one_hot(0)
                    for i in range(NSPLIT):
                        split(n + i)
                    start_of_job()
                    rest_of_job(then_next=False)
            loop.reg = None
            norm_rows(4, 6)

        @block.tensor
        def _(pe):
            loop = Loop()

            def passes(acc, x_hi, x_lo, w_hi, w_lo, start, stop, weights_move):
                for m, (a, b) in enumerate(((x_hi, w_hi), (x_lo, w_hi), (x_hi, w_lo))):
                    lhs, rhs = (a, b) if weights_move else (b, a)
                    ins = pe.matmul(acc, lhs, rhs, start=start and m == 0, stop=stop and m == 2,
                                    skip_group_check=True)
                return ins

            def piece(i, k):
                pe.wait_ge(lo_ready, loop.at("piece", i + 1))
                return (whi[:, i % NSPLIT, :].rearrange("p (k n) -> p k n", k=k),
                        wlo[:, i % NSPLIT, :].rearrange("p (k n) -> p k n", k=k))

            def transpose_rows(q):
                for t in range(TT):
                    pe.wait_ge(y_ready, 2 * q + t + 1)
                    for c in range(KC):
                        ins = pe.transpose(ps[:, 2 * t + c // 4, P * (c % 4):P * (c % 4) + P],
                                           y[:, t, c * P:(c + 1) * P], ident[:])
                    ins.then_inc(xT_ps, 1)

            def transpose_half(q, half, bank):
                for t in range(TT):
                    pe.wait_ge(y_ready, 2 * q + t + 1)
                    for c in range(4):
                        c0 = 512 * half + c * P
                        ins = pe.transpose(ps[:, bank + t, c * P:(c + 1) * P], y[:, t, c0:c0 + P],
                                           ident[:])
                    ins.then_inc(xT_ps, 1)

            def columns_out(i, half, bank):
                hi, lo = piece(i, 4)
                for c in range(4):
                    acc = ps[:, bank + c // 2, 256 * (c % 2):256 * (c % 2) + 256]
                    for k in range(4):
                        kk = 4 * half + k
                        ins = passes(acc, xT_hi[:, kk, :], xT_lo[:, kk, :],
                                     hi[:, k, c * P:(c + 1) * P], lo[:, k, c * P:(c + 1) * P],
                                     start=half == 0 and k == 0 and c % 2 == 0,
                                     stop=half == 1 and k == 3, weights_move=False)
                ins.then_inc(piece_used, 1)

            def tokens_out(i, half, bank):
                hi, lo = piece(i, 4)
                for t in range(TT):
                    s = slice(t * P, (t + 1) * P)
                    for k in range(4):
                        kk = 4 * half + k
                        ins = passes(ps[:, bank + t, :], xT_hi[:, kk, s], xT_lo[:, kk, s],
                                     hi[:, k, :], lo[:, k, :], start=half == 0 and k == 0,
                                     stop=half == 1 and k == 3, weights_move=True)
                ins.then_inc(piece_used, 1)

            def two_rows_out(i, hi_of, lo_of, first, last, chunks=(0, 1)):
                hi, lo = piece(i, 2)
                for kk in chunks:
                    for t in range(TT):
                        for c in range(2):
                            s = slice(c * 512, (c + 1) * 512)
                            ins = passes(ps[:, 4 + 2 * t + c, :], hi_of(kk, t), lo_of(kk, t),
                                         hi[:, kk, s], lo[:, kk, s], start=first and kk == 0,
                                         stop=last and kk == 1, weights_move=True)
                if 1 in chunks:
                    ins.then_inc(piece_used, 1)

            def mixer(l, q):
                n = MIX_BASE[l]
                transpose_rows(q)
                pe.wait_ge(xT_ready, 2 * q + 2)
                pe.wait_ge(wif_ready, 1)
                for t in range(TT):
                    s = slice(t * P, (t + 1) * P)
                    for k in range(KC):
                        w = slice(8 * k, 8 * k + 8)
                        ins = passes(ps[:, 6, 8 * t:8 * t + 8], xT_hi[:, k, s], xT_lo[:, k, s],
                                     wif_hi[:, l, w], wif_lo[:, l, w], start=k == 0, stop=k == KC - 1,
                                     weights_move=True)
                ins.then_inc(gate_ps, 1)

                def gate_transposes():
                    pe.wait_ge(gate_sb, l + 1)
                    for i in range(2):
                        for t in range(TT):
                            c = 256 * i + P * t
                            ins = pe.transpose(ps[0:HM, 7, c:c + P], gate_t[:, t, 4 * i:4 * i + 4],
                                               ident[:])
                    ins.then_inc(grow_ps, 1)

                def conv_parameters():
                    pe.wait_ge(small_in, SMALL)
                    for c in range(KC):
                        ins = pe.transpose(ps[:, 6, 128 + 10 * c:138 + 10 * c],
                                           convrow[:, c * P:(c + 1) * P], ident[0:10, 0:10])
                    ins.then_inc(conv_ps, 1)

                def gate_columns():
                    pe.wait_ge(grows, l + 1)
                    for m, r in ((0, 6), (1, 5)):
                        for t in range(TT):
                            c = 64 + 8 * m + 4 * t
                            ins = pe.transpose(ps[:, 6, c:c + HM], rows[r][:, t * P:(t + 1) * P],
                                               ident[0:HM, 0:HM])
                    ins.then_inc(gcol_ps, 1)

                def head_scores(hd):
                    k = 4 * l + hd
                    if hd == 0:
                        pe.wait_ge(silu_done, 2 * (l + 1))
                        pe.wait_ge(gcol, l + 1)
                        pe.wait_ge(proj_out, 7 * l + VM + 1)
                    else:
                        pe.wait_ge(decay_ready, 2 * k)
                    pe.matmul(ps[:, 2, 0:256], sel[:, hd, :], rows[7], start=True, stop=False,
                              skip_group_check=True)
                    pe.matmul(ps[:, 2, 256:384], sel[:, hd, :], rows[7][:, P:], start=False,
                              stop=False, skip_group_check=True)
                    pe.matmul(ps[:, 2, 0:P], ident_b[:], mask_m[:], start=False, stop=True,
                              skip_group_check=True)
                    pe.matmul(ps[:, 2, 256:384], ident_b[:], mask_m[:], start=False, stop=True,
                              skip_group_check=True).then_inc(head_ps, 1)
                    if hd:
                        pe.wait_ge(pT_ready, k)
                    pe.matmul(ps[:, 3, 0:256], qkc[:, 4 + hd, 0:P], qkc[:, hd, :], start=True,
                              stop=True, skip_group_check=True)
                    pe.matmul(ps[:, 3, 256:384], qkc[:, 4 + hd, P:], qkc[:, hd, P:], start=True,
                              stop=True, skip_group_check=True).then_inc(head_ps, 1)

                def head_values(hd):
                    k = 4 * l + hd
                    pe.wait_ge(pT_ready, k + 1)
                    if hd < 2:
                        pe.wait_ge(proj_out, 7 * (l + 1))
                    else:
                        pe.wait_ge(num_out, 4 * (k - 1))
                    w = DHM + 1
                    acc = ps[:, hd % 2, :]
                    pe.matmul(acc[:, 0:w], pT[:, hd % 2, 0:P], vm[:, 0, hd, 0:w], start=True,
                              stop=True, skip_group_check=True)
                    pe.matmul(acc[:, 130:130 + w], pT[:, hd % 2, P:2 * P], vm[:, 0, hd, 0:w],
                              start=True, stop=False, skip_group_check=True)
                    pe.matmul(acc[:, 130:130 + w], pT[:, hd % 2, 2 * P:], vm[:, 1, hd, 0:w],
                              start=False, stop=True, skip_group_check=True).then_inc(num_ps, 1)

                def pair_scores(p):
                    if p == 0:
                        pe.wait_ge(proj_out, 7 * l + KS + 1)
                    for a in range(2):
                        s = slice(64 * a, 64 * a + 64)
                        z = ps[:, 4 + a, :]
                        pe.matmul(z[:, 0:256], ksT[s, p, 0:P], qsT[s, p, :], start=True, stop=False,
                                  skip_group_check=True)
                        pe.matmul(z[:, 256:384], ksT[s, p, P:], qsT[s, p, P:], start=False,
                                  stop=False, skip_group_check=True)
                        for c in (0, 256):
                            ins = pe.matmul(z[:, c:c + P], ident_b[:], mask_s[:], start=False,
                                            stop=False, skip_group_check=True)
                    ins.then_inc(z_ps, 1)

                def pair_sums(p):
                    pe.wait_ge(softp_ready, 4 * l + p + 1)
                    for a in range(2):
                        z = ps[:, 4 + a, :]
                        pe.matmul(z[:, 0:256], tri_neg[:], softp[:, a, 0:256], start=False, stop=False,
                                  skip_group_check=True)
                        pe.matmul(z[:, P:256], neg1[:], softp[:, a, 256:384], start=False, stop=True,
                                  skip_group_check=True)
                        ins = pe.matmul(z[:, 256:384], tri_neg[:], softp[:, a, 256:384], start=False,
                                        stop=True, skip_group_check=True)
                    ins.then_inc(sum_ps, 1)

                def pair_values(p):
                    pe.wait_ge(aT_ready, 4 * l + p + 1)
                    if p == 0:
                        pe.wait_ge(proj_out, 7 * l + VS + 1)
                    else:
                        pe.wait_ge(av_out, 4 * l + p)
                    for a in range(2):
                        s = slice(64 * (2 * p + a), 64 * (2 * p + a) + 64)
                        o0, o1 = slice(64 * a, 64 * a + 64), slice(P + 64 * a, P + 64 * a + 64)
                        pe.matmul(ps[:, 7, o0], aT[:, a, 0:P], vs[:, 0, s], start=True, stop=True,
                                  skip_group_check=True)
                        pe.matmul(ps[:, 7, o1], aT[:, a, P:256], vs[:, 0, s], start=True, stop=False,
                                  skip_group_check=True)
                        ins = pe.matmul(ps[:, 7, o1], aT[:, a, 256:384], vs[:, 1, s], start=False,
                                        stop=True, skip_group_check=True)
                    ins.then_inc(av_ps, 1)

                for b in range(BLOCKS):
                    if b >= 2:
                        pe.wait_ge(proj_out, 7 * l + b - 1)
                    for half in range(2):
                        i = 2 * b + half
                        out_of = tokens_out if b in (VS, VM, OM) else columns_out
                        out_of(n + i, half, 2 * (b % 2))
                        if i == 0:
                            gate_transposes()
                            if l == 0:
                                conv_parameters()
                        if i == 3:
                            gate_columns()
                        if i % 2 == 0 and 6 <= i <= 12:
                            pair_values(i // 2 - 3)
                        if i % 2 == 0 and 4 <= i <= 10:
                            pair_scores(i // 2 - 2)
                        if i % 2 == 1 and 5 <= i <= 11:
                            pair_sums(i // 2 - 2)
                        if i == 12:
                            head_scores(0)
                head_scores(1)
                head_values(0)

                def out_rows(i, chunks=(0, 1)):
                    c0 = 2 * OUT_PIECES[i]
                    two_rows_out(n + 2 * BLOCKS + i,
                                 lambda kk, t: xT_hi[:, c0 + kk, t * P:(t + 1) * P],
                                 lambda kk, t: xT_lo[:, c0 + kk, t * P:(t + 1) * P],
                                 first=i == 0, last=i == 3, chunks=chunks)

                transpose_half(q + 1, 1, 4)
                head_scores(2)
                head_values(1)
                pe.wait_ge(xT_ready, 2 * (q + 1) + 2)
                out_rows(0, (0,))
                head_scores(3)
                head_values(2)
                out_rows(0, (1,))
                head_values(3)
                out_rows(1)
                transpose_half(q + 2, 0, 0)
                pe.wait_ge(xT_ready, 2 * (q + 2) + 2)
                out_rows(2)
                out_rows(3)

            pe.wait_ge(consts, CONSTS)
            mixer(0, 0)

            transpose_rows(3)
            pe.wait_ge(xT_ready, 8)
            n = FFN_BASE

            def gate_up(i):
                for half in range(2):
                    columns_out(i + half, half, 0)
                for half in range(2):
                    columns_out(i + 2 + half, half, 2)

            def down(i, f):
                pe.wait_ge(hid_ready, loop.at("block", f + 1))
                for half in range(2):
                    def part(v):
                        hv = v[:, f % 2, :].rearrange("p (k t) -> p k t", k=4)
                        return lambda kk, t: hv[:, 2 * half + kk, t * P:(t + 1) * P]
                    two_rows_out(i + half, part(hid_hi), part(hid_lo), first=False, last=False)

            gate_up(n)
            for b in range(4, 8):
                for c in range(4):
                    pe.matmul(ps[:, b, c * P:(c + 1) * P], zero_b[:], zero_b[:], start=c == 0,
                              stop=False, skip_group_check=True)
            with pe.Fori(0, (DENSE_FULL - 1) // 2) as r:
                loop.reg, loop.per = r, {"piece": 12, "block": 2}
                for f in (1, 2):
                    pe.wait_ge(prod_ready, loop.at("block", f))
                    gate_up(n + 4 + 6 * (f - 1))
                    down(n + 8 + 6 * (f - 1), f - 1)
            loop.reg = None
            n += 6 * DENSE_FULL - 2
            pe.wait_ge(prod_ready, DENSE_FULL)
            for m in range(2):
                pe.wait_ge(lo_ready, n + 1)
                hi = whi[:, n % NSPLIT, 0:KC * TAIL].rearrange("p (k n) -> p k n", k=KC)
                lo = wlo[:, n % NSPLIT, 0:KC * TAIL].rearrange("p (k n) -> p k n", k=KC)
                for c in range(2):
                    s = slice(64 * c, 64 * c + P)
                    for k in range(KC):
                        ins = passes(ps[:, 2 * m, 256 * c:256 * c + 256], xT_hi[:, k, :],
                                     xT_lo[:, k, :], hi[:, k, s], lo[:, k, s], start=k == 0,
                                     stop=k == KC - 1, weights_move=False)
                ins.then_inc(piece_used, 1)
                n += 1
            down(n, DENSE_FULL - 1)
            n += 2
            pe.wait_ge(hid_ready, DENSE_FULL + 1)
            hi, lo = piece(n, 2)
            hv = [v[:, DENSE_FULL % 2, 0:512].rearrange("p (k t) -> p k t", k=2)
                  for v in (hid_hi, hid_lo)]
            for kk, k0 in ((0, 0), (1, 64)):
                for t in range(TT):
                    ts = slice(t * P, (t + 1) * P)
                    for c in range(2):
                        s = slice(c * 512, (c + 1) * 512)
                        ins = passes(ps[:, 4 + 2 * t + c, :], hv[0][k0:, kk, ts], hv[1][k0:, kk, ts],
                                     hi[k0:, kk, s], lo[k0:, kk, s], start=False, stop=kk == 1,
                                     weights_move=True)
            ins.then_inc(piece_used, 1)
            mixer(1, 4)

            transpose_rows(7)
            pe.wait_ge(xT_hi_ready, 16)
            for t in range(TT):
                for k in range(KC):
                    ins = pe.matmul(ps[:, 4, 8 * t:8 * t + 8], xT_f[:, k, t * P:(t + 1) * P],
                                    wr[:, k, :], start=k == 0, stop=k == KC - 1,
                                    skip_group_check=True)
            ins.then_inc(route_ps, 1)
            pe.wait_ge(chosen, 1)
            ch = rt[:, 14]
            pe.matmul(ps[:, 5, 0:8], tri[:], ch[:, 0], start=True, stop=True, skip_group_check=True)
            pe.matmul(ps[:, 5, 8:16], ones[:, 0:P], ch[:, 0], start=True, stop=False,
                      skip_group_check=True)
            pe.matmul(ps[:, 5, 8:16], tri[:], ch[:, 1], start=False, stop=True, skip_group_check=True)
            for t in range(TT):
                ins = pe.matmul(ps[:, 5, 16:24], ones[:, 0:P], ch[:, t], start=t == 0, stop=t == 1,
                                skip_group_check=True)
            ins.then_inc(count_ps, 1)

            pe.wait_ge(table_ready, 1)
            jobs = pe.value_load(table_i[0:1, 3:4], min_val=E, max_val=JOBS)
            n = MOE_BASE

            def gather(o):
                pe.wait_ge(slots_ready, loop.at("tile", TT * (1 + o)))
                for c in range(KC):
                    for t in range(TT):
                        ins = pe.matmul(ps[:, 2 + c // 4, P * (c % 4):P * (c % 4) + P],
                                        y[:, t, c * P:(c + 1) * P], slots[:, t, :],
                                        start=t == 0, stop=t == 1, skip_group_check=True)
                ins.then_inc(xg_ps, 1)

            def scatter_matrix():
                for t in range(TT):
                    ins = pe.transpose(ps[:, 6, t * P:(t + 1) * P], slots[:, t, :], ident[:])
                ins.then_inc(scatT_ps, 1)

            def product(i, bank):
                for half in range(2):
                    hi, lo = piece(n + i + half, 4)
                    for k in range(4):
                        kk = 4 * half + k
                        ins = passes(ps[:, bank, :], xT_hi[:, kk, 0:P], xT_lo[:, kk, 0:P],
                                     hi[:, k, :], lo[:, k, :], start=half == 0 and k == 0,
                                     stop=half == 1 and k == 3, weights_move=True)
                    ins.then_inc(piece_used, 1)

            def hid_transpose(f):
                pe.wait_ge(e_prod, loop.at("block", f + 1))
                if f >= 2:
                    pe.wait_ge(e_hid, loop.at("block", f - 1))
                for k in range(4):
                    ins = pe.transpose(ps[:, 4 + f % 2, k * P:(k + 1) * P],
                                       prod[:, k * P:(k + 1) * P], ident[:])
                ins.then_inc(e_hidT, 1)

            def down_job(f):
                pe.wait_ge(e_hid, loop.at("block", f + 1))
                for half in range(2):
                    hi, lo = piece(n + down_piece(f, half, EB), 2)
                    for kk in range(2):
                        hs = slice((2 * half + kk) * P, (2 * half + kk + 1) * P)
                        for c in range(2):
                            s = slice(c * 512, (c + 1) * 512)
                            ins = passes(ps[:, 6 + c, :], hid_hi[:, f % 2, hs],
                                         hid_lo[:, f % 2, hs], hi[:, kk, s], lo[:, kk, s],
                                         start=f == 0 and half == 0 and kk == 0,
                                         stop=f == EB - 1 and half == 1 and kk == 1,
                                         weights_move=True)
                    ins.then_inc(piece_used, 1)

            def scatter():
                pe.wait_ge(o_ready, loop.at("job", 1))
                for t, banks in enumerate(((2, 3), (4, 5))):
                    for c in range(2):
                        pe.matmul(ps[:, banks[c], :], scatT[:, t, :], o_hi[:, c, :], start=True,
                                  stop=False, skip_group_check=True)
                        ins = pe.matmul(ps[:, banks[c], :], scatT[:, t, :], o_lo[:, c, :],
                                        start=False, stop=True, skip_group_check=True)
                ins.then_inc(scat_ps, 1)

            def start_of_job():
                gather(0)
                scatter_matrix()
                pe.wait_ge(xg_ready, loop.at("job", 1))
                product(0, 0)
                product(2, 1)

            def rest_of_job(then_next):
                for f in range(1, EB):
                    if f == 1:
                        pe.wait_ge(job_done, loop.at("job", 1))
                        pe.wait_ge(scatT_ready, loop.at("job", 1))
                    else:
                        pe.wait_ge(e_prod, loop.at("block", f - 1))
                    product(gate_piece(f, 0), 2 * (f % 2))
                    hid_transpose(f - 1)
                    product(gate_piece(f, 0) + 2, 2 * (f % 2) + 1)
                    down_job(f - 1)
                hid_transpose(EB - 1)
                if then_next:
                    gather(1)
                down_job(EB - 1)
                if then_next:
                    pe.wait_ge(xg_ready, loop.at("job", 2))
                    product(JOB_PIECES, 0)
                scatter()
                if then_next:
                    scatter_matrix()
                    product(JOB_PIECES + 2, 1)

            start_of_job()
            with pe.Fori(0, E - 1) as j:
                loop.reg, loop.per = j, PER_JOB
                rest_of_job(then_next=True)
            loop.reg = E - 1
            rest_of_job(then_next=False)
            with pe.Fori(E, JOBS) as j:
                with pe.If(j < jobs):
                    loop.reg = j
                    pe.wait_ge(job_done, loop.at("job", 1))
                    start_of_job()
                    rest_of_job(then_next=False)


def arrival(i, loop):
    last = FFN_BASE + FFN_PIECES - 1
    more = 16 if i >= last and (i - last) % NRAW == 0 else 0
    n = 16 * (i // NRAW + 1) + more
    return n if loop.reg is None else loop.reg * (16 * (loop.per["piece"] // NRAW)) + n


_INS = ['x', 'norm_mix_g', 'w_in', 'b_igate', 'b_fgate', 'conv_w', 'conv_b', 'g_mlstm', 'g_sb',
        'w_out', 'norm_ffn_g', 'ffn_w_gate', 'ffn_w_up', 'ffn_w_down', 'w_router', 'moe_w_gate',
        'moe_w_up', 'moe_w_down', 'norm_final_g']


def kernel(**inputs):
    import numpy as np
    import concourse.bacc as bacc
    from concourse.bass_utils import run_bass_kernel_spmd

    nc = bacc.Bacc("TRN2", target_bir_lowering=False, num_devices=1)
    arrays, args = {}, []
    for name in _INS:
        a = np.ascontiguousarray(inputs[name])
        arrays[f"in_{name}_dram"] = a
        args.append(nc.dram_tensor(f"in_{name}_dram", a.shape, mybir.dt.from_np(a.dtype),
                                   kind="ExternalInput").ap())
    args.append(nc.dram_tensor("out_dram", (1, TT * P, D), F32, kind="ExternalOutput").ap())
    trunk(nc, *args)
    r = run_bass_kernel_spmd(nc, [arrays], core_ids=[0])
    return r.results[0]["out_dram"]
```

```python
from contextlib import ExitStack

import concourse.bass as bass
from concourse import mybir

F32 = mybir.dt.float32
F32R = mybir.dt.float32r
BF16 = mybir.dt.bfloat16
I32 = mybir.dt.int32
ALU = mybir.AluOpType
ACT = mybir.ActivationFunctionType
AX = mybir.AxisListType

P = 128
TT = 2
D = 1024
KC = D // P
DEPTH = 2
HM, DHM = 4, 128
HS, DHS = 8, 64
CONV_K = 4
DM = HM * DHM
GATES = 4 * DM
SBC = GATES + 2 * HM
F_DENSE = 2752
F_EXPERT = 3584
E = 8
FB = 512
NEG = -1e30
EPS = 1e-6

NRAW = 6
NSPLIT = 3
PIECE = 2048
QS, KS, VS, QM, KM, VM, OM = range(7)
BLOCKS = 7
FIRST_COLUMN = [SBC, SBC + 512, SBC + 1024, 0, DM, 2 * DM, 3 * DM]
OUT_PIECES = (2, 3, 0, 1)
MIX_PIECES = 2 * BLOCKS + 4
DENSE_FULL = F_DENSE // FB
TAIL = F_DENSE - DENSE_FULL * FB
FFN_PIECES = 6 * DENSE_FULL + 3
EB = F_EXPERT // FB
JOB_PIECES = 6 * EB
MIX_BASE = [0, MIX_PIECES + FFN_PIECES]
FFN_BASE = MIX_PIECES
MOE_BASE = 2 * MIX_PIECES + FFN_PIECES
EXTRA = 3
JOBS = E + EXTRA


def gate_piece(f, half):
    return half if f == 0 else 4 + 6 * (f - 1) + half


def down_piece(f, half, blocks):
    return 8 + 6 * f + half if f < blocks - 1 else 6 * blocks - 2 + half


class Loop:

    def __init__(self):
        self.reg, self.per = None, {}

    def at(self, kind, value):
        return value if self.reg is None else self.reg * self.per[kind] + value


def trunk(nc, x, norm_mix_g, w_in, b_igate, b_fgate, conv_w, conv_b, g_mlstm, g_sb, w_out,
          norm_ffn_g, ffn_w_gate, ffn_w_up, ffn_w_down, w_router, moe_w_gate, moe_w_up,
          moe_w_down, norm_final_g, out):
    with ExitStack() as ctx:
        def sb(name, shape, dt=F32):
            return ctx.enter_context(nc.sbuf_tensor(name, shape, dt))

        def sem(name):
            return ctx.enter_context(nc.semaphore(name))

        raw = sb("raw", [P, NRAW, PIECE])
        whi = sb("whi", [P, NSPLIT, PIECE], F32R)
        wlo = sb("wlo", [P, NSPLIT, PIECE], F32R)
        h = sb("h", [P, TT, D])
        y = sb("y", [P, TT, D])
        gains = sb("gains", [P, 2, D])
        xT_hi = sb("xT_hi", [P, KC, TT * P], F32R)
        xT_lo = sb("xT_lo", [P, KC, TT * P], F32R)
        hid_hi = sb("hid_hi", [P, 2, 1024], F32R)
        hid_lo = sb("hid_lo", [P, 2, 1024], F32R)
        scatT = sb("scatT", [P, TT, P], F32R)
        scratch = sb("scratch", [P, 3616])
        qkc = sb("qkc", [P, 8, 256])
        vm = sb("vm", [P, TT, HM, DHM + 2])
        om = sb("om", [P, TT, DM])
        qsT = sb("qsT", [P, 4, 256])
        ksT = sb("ksT", [P, 4, 256])
        vs = sb("vs", [P, TT, 512])
        neg_max = sb("neg_max", [HM, TT * P])
        ident = sb("ident", [P, P])
        ident_b = sb("ident_b", [P, P], BF16)
        zero_b = sb("zero_b", [P, P], BF16)
        mask_m = sb("mask_m", [P, P], BF16)
        mask_s = sb("mask_s", [P, P], BF16)
        tri_neg = sb("tri_neg", [P, P])
        neg1 = sb("neg1", [P, P])
        tri = sb("tri", [P, P])
        ones = sb("ones", [P, 256])
        iota_i = sb("iota_i", [P, P], I32)
        iota = sb("iota", [P, P])
        iota_e = sb("iota_e", [P, E])
        desc_e = sb("desc_e", [P, E])
        sel = sb("sel", [HM, HM, P])
        eps = sb("eps", [P, 1])
        convp = sb("convp", [P, KC, DEPTH * (CONV_K + 1)])
        wif = sb("wif", [P, DEPTH, 64])
        wif_hi = sb("wif_hi", [P, DEPTH, 64], F32R)
        wif_lo = sb("wif_lo", [P, DEPTH, 64], F32R)
        wr = sb("wr", [P, KC, E])
        gbias = sb("gbias", [HM, DEPTH, 2])
        ssq = sb("ssq", [P, 4])
        ssq_eps = sb("ssq_eps", [P, 2])
        rms = sb("rms", [P, 2])
        rstd = sb("rstd", [P, 2])
        acol = sb("acol", [P, TT, HM])
        emcol = sb("emcol", [P, TT, HM])
        den = sb("den", [P, TT, HM])
        msc = sb("msc", [P, 6, TT * HM])
        ssc = sb("ssc", [P, 4, TT * HS])
        rt = sb("rt", [P, 16, TT, E])
        job_pos = sb("job_pos", [P, TT, JOBS])
        job_w = sb("job_w", [P, TT, JOBS])
        ovf = sb("ovf", [P, 8, E])
        table = sb("table", [P, 4])
        table_i = sb("table_i", [1, 4], I32)

        ps = ctx.enter_context(nc.psum_tensor("ps", [P, 8, 512], F32))

        qkp = scratch[:, 0:2080].rearrange("p (c t) -> p c t", c=8)
        convrow = scratch[0:10, 2080:3104]
        zt = scratch[:, 2080:2848].rearrange("p (b t) -> p b t", b=2)
        softp = scratch[:, 2848:3616].rearrange("p (b t) -> p b t", b=2)
        aT = zt
        decay = scratch[:, 0:768].rearrange("p (b t) -> p b t", b=2)
        pT = scratch[:, 768:1536].rearrange("p (b t) -> p b t", b=2)
        squares = scratch[:, 2080:3104].rearrange("p (a t) -> p a t", a=2)
        unused = [scratch[:, c:c + 256].rearrange("p (t d) -> p t d", t=TT)
                  for c in (1536, 1792, 3104, 3360)]
        silu = scratch[:, 0:1024]
        prod = scratch[:, 1024:2048]
        slots = scratch[:, 2048:2304].rearrange("p (a t) -> p a t", a=2)
        o_hi, o_lo = hid_hi[:, :, 512:], hid_lo[:, :, 512:]
        rows = [y[0:HM, r // 2, 256 * (r % 2):256 * (r % 2) + 256] for r in range(4)]
        rows += [om[0:HM, r // 2, 256 * (r % 2):256 * (r % 2) + 256] for r in range(3)]
        rows += [neg_max[:]]
        xT_f = qkc

        arrived = [sem(f"arrived{i}") for i in range(NRAW)]
        hi_ready = sem("hi_ready")
        lo_ready = sem("lo_ready")
        piece_used = sem("piece_used")
        x_in = [sem("x_in0"), sem("x_in1")]
        small_in = sem("small_in")
        first_gain_in = sem("first_gain_in")
        gain_in = [sem("gain_in0"), sem("gain_in1")]
        eps_ready = sem("eps_ready")
        consts = sem("consts")
        vm_ones = sem("vm_ones")
        wif_in = sem("wif_in")
        pool_step = sem("pool_step")
        conv_ps = sem("conv_ps")
        convp_ready = sem("convp_ready")
        wif_hi_ready = sem("wif_hi_ready")
        wif_ready = sem("wif_ready")
        sums_out = sem("sums_out")
        h_ready = sem("h_ready")
        ssq_ready = sem("ssq_ready")
        rms_ready = sem("rms_ready")
        rstd_ready = sem("rstd_ready")
        msum = sem("msum")
        mrms = sem("mrms")
        ssum = sem("ssum")
        srms = sem("srms")
        act_step = sem("act_step")
        dve_step = sem("dve_step")
        y_first = sem("y_first")
        y_ready = sem("y_ready")
        xT_ps = sem("xT_ps")
        xT_hi_ready = sem("xT_hi_ready")
        xT_ready = sem("xT_ready")
        proj_out = sem("proj_out")
        conv_done = sem("conv_done")
        silu_done = sem("silu_done")
        om_ready = sem("om_ready")
        grow_ps = sem("grow_ps")
        fabs = sem("fabs")
        flog = sem("flog")
        grows = sem("grows")
        gcol_ps = sem("gcol_ps")
        gcol = sem("gcol")
        head_ps = sem("head_ps")
        decay_ready = sem("decay_ready")
        pT_ready = sem("pT_ready")
        num_ps = sem("num_ps")
        num_out = sem("num_out")
        z_ps = sem("z_ps")
        lnz_ready = sem("lnz_ready")
        softp_ready = sem("softp_ready")
        sum_ps = sem("sum_ps")
        aT_ready = sem("aT_ready")
        av_ps = sem("av_ps")
        av_out = sem("av_out")
        sil_ready = sem("sil_ready")
        prod_ready = sem("prod_ready")
        hid_hi_ready = sem("hid_hi_ready")
        hid_ready = sem("hid_ready")
        route_ps = sem("route_ps")
        rexp_in = sem("rexp_in")
        rexp = sem("rexp")
        chosen = sem("chosen")
        count_ps = sem("count_ps")
        table_ready = sem("table_ready")
        slots_ready = sem("slots_ready")
        scatT_ps = sem("scatT_ps")
        scatT_ready = sem("scatT_ready")
        xg_ps = sem("xg_ps")
        xg_hi_ready = sem("xg_hi_ready")
        xg_ready = sem("xg_ready")
        e_sil = sem("e_sil")
        e_prod = sem("e_prod")
        e_hidT = sem("e_hidT")
        e_hid_hi = sem("e_hid_hi")
        e_hid = sem("e_hid")
        o_sum = sem("o_sum")
        o_hi_ready = sem("o_hi_ready")
        o_ready = sem("o_ready")
        scat_ps = sem("scat_ps")
        tile0_done = sem("tile0_done")
        job_done = sem("job_done")
        stored = sem("stored")

        block = ctx.enter_context(nc.Block())
        Y_MIX, Y_FFN, Y_ROUTE, Y_FINAL = (0, 8), 6, 14, 16
        X_MIX, X_FFN, X_ROUTE = (0, 6), 4, 10
        PER_JOB = {"piece": JOB_PIECES, "block": EB, "job": 1, "tile": TT, "half": 2}

        @block.sync
        def _(sp):
            loop = Loop()

            def load(i, parts):
                if loop.reg is not None or i >= NRAW:
                    sp.wait_ge(lo_ready, loop.at("piece", i - NRAW + 1))
                for place, src in parts:
                    sp.dma_start(place, src).then_inc(arrived[i % NRAW], 16)

            def cols(i, w, half, c0, n=FB):
                v = raw[:, i % NRAW, :].rearrange("p (k n) -> p k n", k=4)
                rows_ = w[half * 512:(half + 1) * 512, bass.ds(c0, n)]
                load(i, [(v, rows_.rearrange("(k p) n -> p k n", p=P))])

            def two_rows(i, w, r0):
                v = raw[:, i % NRAW, :].rearrange("p (k n) -> p k n", k=2)
                load(i, [(v, w[bass.ds(r0, 256), :].rearrange("(k p) n -> p k n", p=P))])

            def mixer(l):
                n = MIX_BASE[l]
                for b in range(BLOCKS):
                    for half in range(2):
                        cols(n + 2 * b + half, w_in[l], half, FIRST_COLUMN[b])
                for i in range(4):
                    two_rows(n + 2 * BLOCKS + i, w_out[l], 256 * OUT_PIECES[i])

            for t in range(TT):
                sp.dma_start(h[:, t, :], x[0, t * P:(t + 1) * P, :]).then_inc(x_in[t], 16)
            mixer(0)
            n = FFN_BASE
            wg, wu, wd = ffn_w_gate[0], ffn_w_up[0], ffn_w_down[0]
            for half in range(2):
                cols(n + half, wg, half, 0)
            for half in range(2):
                cols(n + 2 + half, wu, half, 0)
            with sp.Fori(0, DENSE_FULL - 1) as r:
                loop.reg, loop.per = r, {"piece": 6}
                for half in range(2):
                    cols(n + 4 + half, wg, half, (r + 1) * FB)
                for half in range(2):
                    cols(n + 6 + half, wu, half, (r + 1) * FB)
                for half in range(2):
                    two_rows(n + 8 + half, wd, r * FB + 256 * half)
            loop.reg = None
            n += 6 * DENSE_FULL - 2
            c0 = DENSE_FULL * FB
            for w in (wg, wu):
                v = raw[:, n % NRAW, 0:KC * TAIL].rearrange("p (k n) -> p k n", k=KC)
                load(n, [(v, w[:, c0:].rearrange("(k p) n -> p k n", p=P))])
                n += 1
            for half in range(2):
                two_rows(n, wd, c0 - FB + 256 * half)
                n += 1
            v = raw[:, n % NRAW, :].rearrange("p (k n) -> p k n", k=2)
            load(n, [(v[:, 0], wd[c0:c0 + P, :]), (v[:, 1], wd[F_DENSE - P:, :])])
            mixer(1)

            def job(e):
                n = MOE_BASE

                def expert(w):
                    return w[0, bass.ds(e, 1)].rearrange("e r c -> (e r) c")

                for f in range(EB):
                    for w, o in ((moe_w_gate, 0), (moe_w_up, 2)):
                        for half in range(2):
                            cols(n + gate_piece(f, half) + o, expert(w), half, f * FB)
                    if f:
                        for half in range(2):
                            two_rows(n + down_piece(f - 1, half, EB), expert(moe_w_down),
                                     (f - 1) * FB + 256 * half)
                for half in range(2):
                    two_rows(n + down_piece(EB - 1, half, EB), expert(moe_w_down),
                             (EB - 1) * FB + 256 * half)

            with sp.Fori(0, E) as j:
                loop.reg, loop.per = j, {"piece": JOB_PIECES}
                job(j)
            sp.wait_ge(table_ready, 1)
            jobs = sp.value_load(table_i[0:1, 3:4], min_val=E, max_val=JOBS)
            with sp.Fori(E, JOBS) as j:
                loop.reg = j
                with sp.If(j < jobs):
                    e = sp.value_load(table_i[0:1, bass.ds(j - E, 1)], min_val=0, max_val=E - 1)
                    job(e)
            loop.reg = None
            for t in range(TT):
                sp.wait_ge(y_ready, Y_FINAL + t + 1)
                sp.dma_start(out[0, t * P:(t + 1) * P, :], y[:, t, :]).then_inc(stored, 16)
            sp.wait_ge(stored, 16 * TT)

        @block.gpsimd
        def _(pool):
            steps = [0]

            def step(ins):
                steps[0] += 1
                ins.then_inc(pool_step, 1)

            pool.memset(eps[:], EPS).then_inc(eps_ready, 1)
            for t, v in ((ident, 0.0), (ident_b, 0.0), (mask_m, 0.0), (mask_s, 0.0),
                         (tri_neg, -1.0), (tri, 1.0), (sel, 0.0)):
                step(pool.memset(t[:], v))
            pool.iota(iota_i[:], [[1, P]], base=0, channel_multiplier=0).then_inc(pool_step, 1)
            pool.memset(neg1[:], -1.0).then_inc(consts, 1)
            pool.memset(ones[:], 1.0).then_inc(consts, 1)
            pool.memset(zero_b[:], 0.0).then_inc(consts, 1)
            pool.wait_ge(pool_step, steps[0] + 1)
            for t in (ident, ident_b):
                pool.affine_select(out=t[:], in_=t[:], compare_op=ALU.not_equal, fill=1.0, base=0,
                                   pattern=[[-1, P]], channel_multiplier=1).then_inc(consts, 1)
            for t, base in ((mask_m, 0), (mask_s, -1)):
                pool.affine_select(out=t[:], in_=t[:], compare_op=ALU.is_ge, fill=NEG, base=base,
                                   pattern=[[1, P]], channel_multiplier=-1).then_inc(consts, 1)
            pool.affine_select(out=tri_neg[:], in_=tri_neg[:], compare_op=ALU.is_ge, fill=0.0,
                               base=0, pattern=[[-1, P]], channel_multiplier=1).then_inc(consts, 1)
            pool.affine_select(out=tri[:], in_=tri[:], compare_op=ALU.is_ge, fill=0.0,
                               base=-1, pattern=[[1, P]], channel_multiplier=-1).then_inc(consts, 1)
            pool.affine_select(out=sel[:], in_=sel[:], compare_op=ALU.not_equal, fill=1.0, base=0,
                               pattern=[[-1, HM], [0, P]], channel_multiplier=1).then_inc(consts, 1)
            pool.tensor_copy(iota[:], iota_i[:]).then_inc(consts, 1)
            pool.wait_ge(consts, 11)
            pool.tensor_copy(iota_e[:], iota[:, 0:E]).then_inc(consts, 1)
            pool.tensor_scalar(desc_e[:], iota[:, 0:E], -1.0, float(E), ALU.mult, ALU.add
                               ).then_inc(consts, 1)
            pool.memset(vm[:], 1.0).then_inc(vm_ones, 1)
            for l in range(DEPTH):
                r0 = l * (CONV_K + 1)
                pool.dma_start(convrow[r0:r0 + CONV_K, :], conv_w[l]).then_inc(small_in, 16)
                pool.dma_start(convrow[r0 + CONV_K:r0 + CONV_K + 1, :],
                               conv_b[l:l + 1, :]).then_inc(small_in, 16)
                for i, b in enumerate((b_igate, b_fgate)):
                    pool.dma_start(gbias[:, l, i:i + 1],
                                   b[l].rearrange("(h o) -> h o", o=1)).then_inc(small_in, 16)
            pool.dma_start(wr[:], w_router[0].rearrange("(k p) e -> p k e", p=P)).then_inc(small_in, 16)

            def gain(u, *parts):
                if u >= 2:
                    pool.wait_ge(y_ready, 2 * (0, 0, 1, 3, 4, 5, 7)[u])
                c = 0
                for g in parts:
                    n = g.shape[-1]
                    pool.dma_start(gains[:, u % 2, c:c + n],
                                   g.rearrange("(a n) -> a n", a=1).to_broadcast([P, n])
                                   ).then_inc(gain_in[u % 2], 16)
                    c += n

            gain(1, g_mlstm[0], g_sb[0])
            gain(2, norm_ffn_g[0])
            gain(3, norm_mix_g[1])
            gain(4, g_mlstm[1], g_sb[1])
            gain(5, norm_ffn_g[1])
            gain(6, norm_final_g)
        CONSTS = 13
        SMALL = 16 * 9

        @block.scalar
        def _(act):
            loop = Loop()
            done = [0]
            steps = [0]

            def own(ins):
                steps[0] += 1
                ins.then_inc(act_step, 1)
                act.wait_ge(act_step, steps[0])

            def split(i):
                act.wait_ge(arrived[i % NRAW], arrival(i, loop))
                if loop.reg is not None or i >= NSPLIT:
                    act.wait_ge(piece_used, loop.at("piece", i - NSPLIT + 1))
                act.activation(whi[:, i % NSPLIT, :], raw[:, i % NRAW, :], ACT.Copy
                               ).then_inc(hi_ready, 1)

            def split_upto(i):
                while done[0] <= i:
                    split(done[0])
                    done[0] += 1

            def tables(name):
                act.preload_act_table_set(name)

            def norm_stats(u):
                if u == 4:
                    tables("sqrt_and_others")
                for t in range(TT):
                    for c in range(2):
                        if u == 4:
                            act.wait_ge((tile0_done, job_done)[t], jobs + t)
                        elif u == 0:
                            act.wait_ge(x_in[t], 16)
                        else:
                            act.wait_ge(h_ready, 4 * (u - 1) + 2 * t + c + 1)
                        cs = slice(512 * c, 512 * c + 512)
                        m = 2 * t + c
                        act.activation(y[:, t, cs], h[:, t, cs], ACT.Square, scale=D ** -0.5,
                                       accum_out=ssq[:, m:m + 1]).then_inc(ssq_ready, 1)
                        if c == 0:
                            act.wait_ge(ssq_ready, 3 * (TT * u + t) + 1)
                            act.activation(ssq_eps[:, t:t + 1], ssq[:, m:m + 1], ACT.Identity,
                                           bias=eps[:]).then_inc(ssq_ready, 1)
                    act.wait_ge(ssq_ready, 3 * (TT * u + t) + 3)
                    act.activation(rms[:, t:t + 1], ssq[:, m:m + 1], ACT.Sqrt,
                                   bias=ssq_eps[:, t:t + 1]).then_inc(rms_ready, 1)

            def xT_copy(q):
                for half in range(2):
                    xT_copy_half(q + half, half, 2 * half)

            def xT_copy_half(q, half, bank):
                for t in range(TT):
                    act.wait_ge(xT_ps, 2 * q + t + 1)
                    act.activation(xT_hi[:, 4 * half:4 * half + 4, t * P:(t + 1) * P],
                                   ps[:, bank + t, :].rearrange("p (c t) -> p c t", t=P), ACT.Copy
                                   ).then_inc(xT_hi_ready, 1)

            def mixer(l):
                n, q = MIX_BASE[l], X_MIX[l]
                norm_stats(2 * l)
                if l == 0:
                    act.wait_ge(consts, CONSTS)
                    split_upto(n)
                xT_copy(q)
                if l == 1:
                    split_upto(n + 2)
                else:
                    act.wait_ge(wif_in, 32)
                    act.activation(wif_hi[:], wif[:], ACT.Copy).then_inc(wif_hi_ready, 1)

                def evacuate(b):
                    act.wait_ge(piece_used, n + 2 * b + 2)
                    bank = ps[:, 2 * (b % 2):2 * (b % 2) + 2, :]
                    if b in (QM, KM):
                        g = b - QM
                        ins = act.activation(qkp[:, 4 * g:4 * g + 4, 3:259],
                                             bank.rearrange("p b (c t) -> p (b c) t", t=256), ACT.Copy)
                    elif b == VM:
                        act.wait_ge(vm_ones, 1)
                        for t in range(TT):
                            ins = act.activation(vm[:, t, :, 0:DHM],
                                                 bank[:, t, :].rearrange("p (h d) -> p h d", h=HM),
                                                 ACT.Copy)
                            if t == 0:
                                ins.then_inc(act_step, 1)
                                steps[0] += 1
                    elif b == OM:
                        ins = act.activation(om[:], bank, ACT.Copy)
                    elif b == VS:
                        ins = act.activation(vs[:], bank, ACT.Copy)
                    else:
                        dst = qsT if b == QS else ksT
                        ins = act.activation(dst[:], bank.rearrange("p b (c t) -> p (b c) t", t=256),
                                             ACT.Copy, scale=DHS ** -0.5 if b == QS else 1.0)
                    ins.then_inc(proj_out, 1)

                def gate_rows():
                    act.wait_ge(fabs, l + 1)
                    own(act.activation(rows[3], rows[2], ACT.Exp, scale=-1.0))
                    act.activation(rows[4], rows[3], ACT.Ln, bias=ones[0:HM, 0:1]
                                   ).then_inc(flog, 1)

                def gate_columns():
                    act.wait_ge(gcol_ps, l + 1)
                    v = ps[:, 6, 64:80].rearrange("p (m t h) -> p m t h", m=2, t=TT)
                    act.activation(acol[:], v[:, 0], ACT.Copy).then_inc(gcol, 1)
                    act.activation(emcol[:], v[:, 1], ACT.Exp, scale=-1.0).then_inc(gcol, 1)

                def decays(hd):
                    k = 4 * l + hd
                    if hd == 0:
                        act.wait_ge(gcol, 2 * (l + 1))
                    act.wait_ge(head_ps, 2 * k + 1)
                    if hd >= 2:
                        act.wait_ge(pT_ready, k - 1)
                    for j, s in ((0, slice(0, 256)), (1, slice(256, 384))):
                        act.activation(decay[:, hd % 2, s], ps[:, 2, s], ACT.Exp,
                                       bias=acol[:, j, hd:hd + 1]).then_inc(decay_ready, 1)

                def numerators(hd):
                    act.wait_ge(num_ps, 4 * l + hd + 1)
                    v = ps[:, hd % 2, 0:260].rearrange("p (t d) -> p t d", t=TT)
                    act.activation(y[:, :, hd * P:(hd + 1) * P], v[:, :, 0:P], ACT.Copy
                                   ).then_inc(num_out, 1)
                    act.activation(den[:, :, hd:hd + 1], v[:, :, P:P + 1], ACT.Copy
                                   ).then_inc(num_out, 1)
                    for t in range(TT):
                        c = HM * t + hd
                        act.activation(unused[hd][:, t], v[:, t, 0:P], ACT.Square,
                                       accum_out=msc[:, 5, c:c + 1]).then_inc(num_out, 1)

                def soft(p):
                    z = ps[:, 4:6, 0:384]
                    act.wait_ge(z_ps, 4 * l + p + 1)
                    own(act.activation(zt[:], z, ACT.Abs))
                    steps[0] += 1
                    act.activation(zt[:], zt[:], ACT.Exp, scale=-1.0).then_inc(act_step, 1)
                    tables("natural_log")
                    act.wait_ge(act_step, steps[0])
                    act.activation(zt[:], zt[:], ACT.Ln, bias=ones[:, 0:1]).then_inc(lnz_ready, 1)
                    tables("exp_and_others")

                def pair_weights(p):
                    act.wait_ge(sum_ps, 4 * l + p + 1)
                    act.activation(aT[:], ps[:, 4:6, 0:384], ACT.Exp).then_inc(aT_ready, 1)

                def pair_rows(p):
                    act.wait_ge(av_ps, 4 * l + p + 1)
                    c = 512 + p * P
                    act.activation(y[:, :, c:c + P], ps[:, 7, 0:256].rearrange(
                        "p (t d) -> p t d", t=TT), ACT.Copy).then_inc(av_out, 1)

                for b in range(BLOCKS):
                    for half in range(2):
                        i = 2 * b + half
                        if i < 13:
                            split_upto(n + i + 3)
                        if half == 1:
                            evacuate(b)
                        if i == 2 and l == 0:
                            act.wait_ge(conv_ps, 1)
                            act.activation(convp[:], ps[:, 6, 128:208].rearrange(
                                "p (c k) -> p c k", c=KC), ACT.Copy).then_inc(convp_ready, 1)
                        if i == 2:
                            gate_rows()
                            tables("exp_and_others")
                        if i == 5:
                            gate_columns()
                        if i % 2 == 0 and 6 <= i <= 12:
                            pair_rows(i // 2 - 3)
                        if i % 2 == 0 and 4 <= i <= 10:
                            soft(i // 2 - 2)
                        if i % 2 == 1 and 5 <= i <= 11:
                            pair_weights(i // 2 - 2)
                        if i == 11:
                            tables("silu_and_others")
                            for g in range(2):
                                act.wait_ge(conv_done, 4 * l + 2 * g + 2)
                                act.activation(qkc[:, 4 * g:4 * g + 4, :], qkc[:, 4 * g:4 * g + 4, :],
                                               ACT.Silu).then_inc(silu_done, 1)
                            tables("exp_and_others")
                        if i == 12:
                            decays(0)
                            tables("sqrt_and_others")
                            act.wait_ge(ssum, l + 1)
                            act.activation(ssc[:, 1, :], ssc[:, 0, :], ACT.Sqrt, scale=1.0 / DHS,
                                           bias=eps[:]).then_inc(srms, 1)
                            tables("exp_and_others")

                decays(1)
                numerators(0)
                xT_copy_half(q + 2, 1, 4)
                decays(2)
                numerators(1)
                split_upto(n + 2 * BLOCKS + 2)
                decays(3)
                tables("sigmoid_and_others")
                act.wait_ge(proj_out, 7 * (l + 1))
                act.activation(om[:], om[:], ACT.Sigmoid).then_inc(om_ready, 1)
                numerators(2)
                numerators(3)
                tables("sqrt_and_others")
                act.wait_ge(msum, l + 1)
                act.activation(msc[:, 3, :], msc[:, 2, :], ACT.Sqrt, scale=1.0 / DHM, bias=eps[:]
                               ).then_inc(mrms, 1)
                split_upto(n + 2 * BLOCKS + 3)
                xT_copy_half(q + 3, 0, 0)
                split_upto(n + 2 * BLOCKS + 4)
                split_upto(n + 2 * BLOCKS + 5)

            act.dma_start(gains[:, 0, :], norm_mix_g[0].rearrange("(a n) -> a n", a=1)
                          .to_broadcast([P, D])).then_inc(first_gain_in, 16)
            for l in range(DEPTH):
                act.dma_start(wif[:, l, :].rearrange("p (k c) -> p k c", k=KC),
                              w_in[l][:, GATES:SBC].rearrange("(k p) c -> p k c", p=P)
                              ).then_inc(wif_in, 16)
            tables("sqrt_and_others")
            act.wait_ge(eps_ready, 1)
            mixer(0)

            norm_stats(1)
            xT_copy(X_FFN)
            split_upto(FFN_BASE + 2)
            tables("silu_and_others")

            def gate_silu(f, width=1024):
                act.wait_ge(piece_used, loop.at("piece", FFN_BASE + gate_piece(f, 1) + 1)
                            if f < DENSE_FULL else FFN_BASE + 6 * DENSE_FULL - 1)
                if f:
                    act.wait_ge(prod_ready, loop.at("block", f))
                act.activation(silu[:, 0:width], ps[:, 0:width // 512, :], ACT.Silu
                               ).then_inc(sil_ready, 1)

            def hid_high_dense(f, width=1024):
                act.wait_ge(prod_ready, loop.at("block", f + 1))
                act.activation(hid_hi[:, f % 2, 0:width], prod[:, 0:width], ACT.Copy
                               ).then_inc(hid_hi_ready, 1)

            n = FFN_BASE
            for i in range(4):
                split_upto(n + i + 3)
                if i == 1:
                    gate_silu(0)
            hid_high_dense(0)
            with act.Fori(0, (DENSE_FULL - 1) // 2) as r:
                loop.reg, loop.per = r, {"piece": 12, "block": 2}
                for f in (1, 2):
                    for i in range(6):
                        split(n + 4 + 6 * (f - 1) + i + 3)
                        if i == 1:
                            gate_silu(f)
                        if i == 3:
                            hid_high_dense(f)
            loop.reg = None
            done[0] = n + 4 + 24 + 3
            n += 6 * DENSE_FULL - 2
            for i in range(4):
                split_upto(n + i + 3)
                if i == 0:
                    gate_silu(DENSE_FULL, 512)
                    tables("sqrt_and_others")
                if i == 1:
                    hid_high_dense(DENSE_FULL, 512)
            mixer(1)

            norm_stats(3)
            split_upto(MOE_BASE + 2)
            for half in range(2):
                for t in range(TT):
                    act.wait_ge(xT_ps, 2 * (X_ROUTE + half) + t + 1)
                    act.activation(xT_f[:, 4 * half:4 * half + 4, t * P:(t + 1) * P],
                                   ps[:, 2 * half + t, :].rearrange("p (c t) -> p c t", t=P),
                                   ACT.Copy).then_inc(xT_hi_ready, 1)
            act.wait_ge(rexp_in, 1)
            act.activation(rt[:, 10, :, 0:1], rt[:, 9, :, 0:1], ACT.Exp).then_inc(rexp, 1)

            tables("silu_and_others")
            n = MOE_BASE

            def gathered(o):
                for half in range(2):
                    act.wait_ge(xg_ps, loop.at("half", 2 * o + half + 1))
                    act.activation(xT_hi[:, 4 * half:4 * half + 4, 0:P],
                                   ps[:, 2 + half, :].rearrange("p (c t) -> p c t", t=P),
                                   ACT.Copy).then_inc(xg_hi_ready, 1)

            def scatter_matrix(o):
                act.wait_ge(scatT_ps, loop.at("job", 1 + o))
                act.activation(scatT[:], ps[:, 6, 0:256].rearrange("p (t c) -> p t c", t=TT),
                               ACT.Copy).then_inc(scatT_ready, 1)

            def e_silu(i, f):
                act.wait_ge(piece_used, loop.at("piece", n + i + 1))
                act.activation(silu[:, 0:512], ps[:, 2 * (f % 2), :], ACT.Silu).then_inc(e_sil, 1)

            def hid_high(f):
                act.wait_ge(e_hidT, loop.at("block", f + 1))
                if f >= 2:
                    act.wait_ge(piece_used, loop.at("piece", n + down_piece(f - 2, 1, EB) + 1))
                act.activation(hid_hi[:, f % 2, 0:512], ps[:, 4 + f % 2, :], ACT.Copy
                               ).then_inc(e_hid_hi, 1)

            def rest_of_job(then_next):
                for i in range(4, JOB_PIECES + (4 if then_next else 0)):
                    if i == JOB_PIECES - 4:
                        hid_high(EB - 1)
                    if then_next or i + NSPLIT < JOB_PIECES:
                        split(n + i + NSPLIT)
                    for f in range(1, EB):
                        if i == gate_piece(f, 1):
                            hid_high(f - 1)
                            act.wait_ge(e_prod, loop.at("block", f))
                            e_silu(i, f)
                    if i == JOB_PIECES - 3 and then_next:
                        gathered(1)
                    if i == JOB_PIECES - 1:
                        for c in range(2):
                            if c == 0:
                                act.wait_ge(o_sum, loop.at("job", 1))
                            else:
                                act.wait_ge(piece_used, loop.at("piece", n + JOB_PIECES))
                            act.activation(o_hi[:, c, :], ps[:, 6 + c, :], ACT.Copy
                                           ).then_inc(o_hi_ready, 1)
                    if i == JOB_PIECES + 1:
                        scatter_matrix(1)
                    if i == JOB_PIECES + 3:
                        e_silu(i, 0)

            def start_of_job():
                gathered(0)
                scatter_matrix(0)
                for i in range(4):
                    split(n + i + NSPLIT)
                e_silu(3, 0)

            start_of_job()
            with act.Fori(0, E - 1) as j:
                loop.reg, loop.per = j, PER_JOB
                rest_of_job(then_next=True)
            loop.reg = E - 1
            rest_of_job(then_next=False)
            act.wait_ge(table_ready, 1)
            jobs = act.value_load(table_i[0:1, 3:4], min_val=E, max_val=JOBS)
            with act.Fori(E, JOBS) as j:
                with act.If(j < jobs):
                    loop.reg = j
                    for i in range(NSPLIT):
                        split(n + i)
                    start_of_job()
                    rest_of_job(then_next=False)
            loop.reg = None
            norm_stats(4)

        @block.vector
        def _(dve):
            loop = Loop()
            done = [0]
            steps = [0]

            def own(ins):
                steps[0] += 1
                ins.then_inc(dve_step, 1)
                dve.wait_ge(dve_step, steps[0])

            def both(step):
                for t in range(TT):
                    step(t).then_inc(dve_step, 1)
                steps[0] += TT
                dve.wait_ge(dve_step, steps[0])

            def split(i):
                dve.wait_ge(hi_ready, loop.at("piece", i + 1))
                dve.tensor_tensor(wlo[:, i % NSPLIT, :], raw[:, i % NRAW, :],
                                  whi[:, i % NSPLIT, :].bitcast(F32), ALU.subtract).then_inc(lo_ready, 1)

            def split_upto(i):
                while done[0] <= i:
                    split(done[0])
                    done[0] += 1

            gains_in = [0, 32, 16, 48, 48, 64, 64]

            def norm_rows(k, u):
                if u == 0:
                    dve.wait_ge(first_gain_in, 16)
                else:
                    dve.wait_ge(gain_in[u % 2], gains_in[u])
                for t in range(TT):
                    dve.wait_ge(rms_ready, TT * k + t + 1)
                    dve.reciprocal(rstd[:, t:t + 1], rms[:, t:t + 1]).then_inc(rstd_ready, 1)
                    dve.wait_ge(rstd_ready, TT * k + t + 1)
                    for c in range(2):
                        s = slice(512 * c, 512 * c + 512)
                        dve.scalar_tensor_tensor(y[:, t, s], h[:, t, s], rstd[:, t:t + 1],
                                                 gains[:, u % 2, s], ALU.mult, ALU.mult
                                                 ).then_inc((y_first, y_ready)[c], 1)

            def xT_rest(q):
                for half in range(2):
                    xT_rest_half(q + half, half, 2 * half)

            def xT_rest_half(q, half, bank):
                for t in range(TT):
                    dve.wait_ge(xT_hi_ready, 2 * q + t + 1)
                    v = slice(4 * half, 4 * half + 4), slice(t * P, (t + 1) * P)
                    dve.tensor_tensor(xT_lo[:, v[0], v[1]],
                                      ps[:, bank + t, :].rearrange("p (c t) -> p c t", t=P),
                                      xT_hi[:, v[0], v[1]].bitcast(F32), ALU.subtract
                                      ).then_inc(xT_ready, 1)

            def mixer(l):
                n, q = MIX_BASE[l], X_MIX[l]
                norm_rows(2 * l, 3 * l)
                if l == 0:
                    dve.wait_ge(consts, CONSTS)
                    split_upto(n)
                dve.memset(qkp[:, :, 0:3], 0.0).then_inc(dve_step, 1)
                steps[0] += 1
                xT_rest(q)
                if l == 0:
                    dve.wait_ge(wif_hi_ready, 1)
                    dve.tensor_tensor(wif_lo[:], wif[:], wif_hi[:].bitcast(F32), ALU.subtract
                                      ).then_inc(wif_ready, 1)
                split_upto(n + 2)

                def convolve(g, part):
                    dve.wait_ge(proj_out, 7 * l + QM + g + 1)
                    for tap in range(CONV_K):
                        for j in range(2):
                            c = 4 * g + 2 * part + j
                            w = convp[:, c, 5 * l + tap:5 * l + tap + 1]
                            src = qkp[:, c, tap:tap + 256]
                            if tap == 0:
                                ins = dve.tensor_scalar(qkc[:, c, :], src, w,
                                                        convp[:, c, 5 * l + 4:5 * l + 5],
                                                        ALU.mult, ALU.add)
                            else:
                                dve.wait_ge(dve_step, steps[0] - 1)
                                ins = dve.scalar_tensor_tensor(qkc[:, c, :], src, w, qkc[:, c, :],
                                                               ALU.mult, ALU.add)
                            if (tap, j) == (CONV_K - 1, 1):
                                dve.wait_ge(dve_step, steps[0])
                                ins.then_inc(conv_done, 1)
                            else:
                                ins.then_inc(dve_step, 1)
                                steps[0] += 1

                def gate_rows():
                    dve.wait_ge(grow_ps, l + 1)
                    dve.wait_ge(small_in, SMALL)
                    for i in range(2):
                        own(dve.tensor_scalar(rows[i], ps[0:HM, 7, 256 * i:256 * i + 256],
                                              gbias[:, l, i:i + 1], None, ALU.add))
                    dve.scalar_tensor_tensor(rows[2], rows[1], -1.0, rows[1], ALU.mult, ALU.max
                                             ).then_inc(fabs, 1)
                    dve.wait_ge(flog, l + 1)
                    own(dve.scalar_tensor_tensor(rows[5], rows[1], 0.0, rows[4],
                                                 ALU.min, ALU.subtract))
                    own(dve.tensor_tensor_scan(rows[2], ones[0:HM, :], rows[5], 0.0,
                                               ALU.mult, ALU.add))
                    own(dve.tensor_tensor(rows[6], rows[0], rows[2], ALU.subtract))
                    own(dve.tensor_tensor_scan(rows[3], rows[6], rows[6], NEG,
                                               ALU.max, ALU.max))
                    own(dve.tensor_tensor(rows[5], rows[3], rows[2], ALU.add))
                    dve.tensor_scalar(rows[7], rows[3], -1.0, None, ALU.mult
                                      ).then_inc(grows, 1)

                def weights(hd):
                    k = 4 * l + hd
                    dve.wait_ge(head_ps, 2 * k + 2)
                    dve.wait_ge(decay_ready, 2 * k + 2)
                    if hd >= 2:
                        dve.wait_ge(num_ps, k - 1)
                    dve.scalar_tensor_tensor(pT[:, hd % 2, :], ps[:, 3, 0:384], DHM ** -0.5,
                                             decay[:, hd % 2, :], ALU.mult, ALU.mult
                                             ).then_inc(pT_ready, 1)

                def soft(p):
                    k = 4 * l + p
                    dve.wait_ge(lnz_ready, k + 1)
                    if p:
                        dve.wait_ge(sum_ps, k)
                    dve.scalar_tensor_tensor(softp[:], ps[:, 4:6, 0:384], 0.0, zt[:], ALU.max,
                                             ALU.add).then_inc(softp_ready, 1)

                u = 3 * l + 1
                g = gains[:, u % 2, :]

                def stick_norm():
                    dve.wait_ge(av_out, 4 * (l + 1))
                    own(dve.tensor_tensor(squares[:], y[:, :, 512:], y[:, :, 512:], ALU.mult))
                    for t in range(TT):
                        ins = dve.tensor_reduce(ssc[:, 0, HS * t:HS * t + HS],
                                                squares[:, t, :].rearrange("p (h d) -> p h d", h=HS),
                                                AX.X, ALU.add)
                        if t == 0:
                            own(ins)
                    ins.then_inc(ssum, 1)
                    dve.wait_ge(srms, l + 1)
                    own(dve.reciprocal(ssc[:, 2, :], ssc[:, 1, :]))
                    dve.wait_ge(gain_in[u % 2], gains_in[u])
                    for t in range(TT):
                        ys = y[:, t, 512:].rearrange("p (h d) -> p h d", h=HS)
                        own(dve.tensor_tensor(ys, ys, spread(ssc[:, 2, HS * t:HS * t + HS], DHS),
                                              ALU.mult))
                        dve.tensor_tensor(y[:, t, 512:], y[:, t, 512:], g[:, 512:], ALU.mult
                                          ).then_inc(y_ready, 1)

                for b in range(BLOCKS):
                    for half in range(2):
                        i = 2 * b + half
                        if i < 13:
                            split_upto(n + i + 3)
                        if i == 2:
                            gate_rows()
                        if i == 8:
                            dve.wait_ge(convp_ready, 1)
                            convolve(0, 0)
                        if i == 10:
                            convolve(1, 0)
                        if i % 2 == 0 and 4 <= i <= 10:
                            soft(i // 2 - 2)
                        if i in (8, 10):
                            convolve(i // 2 - 4, 1)
                        if i == 12:
                            weights(0)
                            stick_norm()

                weights(1)
                xT_rest_half(q + 2, 1, 4)
                weights(2)
                split_upto(n + 2 * BLOCKS + 2)
                weights(3)
                dve.wait_ge(om_ready, l + 1)
                for t in range(TT):
                    own(dve.tensor_tensor(om[:, t, :], om[:, t, :], g[:, 0:512], ALU.mult))
                dve.wait_ge(num_out, 16 * (l + 1))
                dve.wait_ge(gcol, 2 * (l + 1))
                flat = den[:].rearrange("p t h -> p (t h)")
                own(dve.scalar_tensor_tensor(msc[:, 0, :], flat, -1.0, flat, ALU.mult, ALU.max))
                own(dve.tensor_tensor(msc[:, 0, :], msc[:, 0, :],
                                      emcol[:].rearrange("p t h -> p (t h)"), ALU.max))
                own(dve.reciprocal(msc[:, 1, :], msc[:, 0, :]))
                own(dve.tensor_tensor(msc[:, 2, :], msc[:, 5, :], msc[:, 1, :], ALU.mult))
                dve.tensor_tensor(msc[:, 2, :], msc[:, 2, :], msc[:, 1, :], ALU.mult).then_inc(msum, 1)
                dve.wait_ge(mrms, l + 1)
                own(dve.reciprocal(msc[:, 4, :], msc[:, 3, :]))
                own(dve.tensor_tensor(msc[:, 4, :], msc[:, 4, :], msc[:, 1, :], ALU.mult))
                for t in range(TT):
                    for hd in range(HM):
                        s = slice(hd * P, (hd + 1) * P)
                        ins = dve.scalar_tensor_tensor(y[:, t, s], y[:, t, s],
                                                       msc[:, 4, HM * t + hd:HM * t + hd + 1],
                                                       om[:, t, s], ALU.mult, ALU.mult)
                    ins.then_inc(y_ready, 1)
                xT_rest_half(q + 3, 0, 0)
                split_upto(n + 2 * BLOCKS + 3)
                split_upto(n + 2 * BLOCKS + 4)
                add_rows(n + MIX_PIECES, 2 * l + 1)

            def spread(v, n):
                return v.rearrange("p (h o) -> p h o", o=1).to_broadcast([P, v.shape[1], n])

            def add_rows(used, k):
                for m in range(4):
                    if m < 3:
                        dve.wait_ge(sums_out, 3 * (k - 1) + m + 1)
                    else:
                        dve.wait_ge(piece_used, used)
                    part = h[:, m // 2, 512 * (m % 2):512 * (m % 2) + 512]
                    dve.tensor_tensor(part, part, ps[:, 4 + m, :], ALU.add).then_inc(h_ready, 1)

            mixer(0)

            norm_rows(1, 2)
            xT_rest(X_FFN)
            split_upto(FFN_BASE + 2)

            def hidden(f, width=1024):
                dve.wait_ge(piece_used, loop.at("piece", FFN_BASE + gate_piece(f, 1) + 3)
                            if f < DENSE_FULL else FFN_BASE + 6 * DENSE_FULL)
                dve.wait_ge(sil_ready, loop.at("block", f + 1))
                dve.tensor_tensor(prod[:, 0:width], silu[:, 0:width],
                                  ps[:, 2:2 + width // 512, :].rearrange("p b c -> p (b c)"), ALU.mult
                                  ).then_inc(prod_ready, 1)
                dve.wait_ge(hid_hi_ready, loop.at("block", f + 1))
                dve.tensor_tensor(hid_lo[:, f % 2, 0:width], prod[:, 0:width],
                                  hid_hi[:, f % 2, 0:width].bitcast(F32), ALU.subtract
                                  ).then_inc(hid_ready, 1)

            n = FFN_BASE
            for i in range(4):
                split_upto(n + i + 3)
            hidden(0)
            with dve.Fori(0, (DENSE_FULL - 1) // 2) as r:
                loop.reg, loop.per = r, {"piece": 12, "block": 2}
                for f in (1, 2):
                    for i in range(6):
                        split(n + 4 + 6 * (f - 1) + i + 3)
                        if i == 3:
                            hidden(f)
            loop.reg = None
            done[0] = n + 4 + 24 + 3
            n += 6 * DENSE_FULL - 2
            for i in range(3):
                split_upto(n + i + 3)
                if i == 1:
                    hidden(DENSE_FULL, 512)
            add_rows(n + 5, 2)
            mixer(1)

            norm_rows(3, 5)
            split_upto(MOE_BASE + 2)
            dve.wait_ge(route_ps, 1)
            both(lambda t: dve.tensor_copy(rt[:, 0, t], ps[:, 4 + 2 * t, 0:E]))
            for c in range(2):
                logit, best, hit, pick = 5 * c, 5 * c + 1, 5 * c + 2, 5 * c + 3
                if c:
                    own(dve.scalar_tensor_tensor(rt[:, 5], rt[:, 3], -3e38, rt[:, 0],
                                                 ALU.mult, ALU.add))
                    own(dve.tensor_scalar(rt[:, 5], rt[:, 5], -3e38, None, ALU.max))
                own(dve.tensor_reduce(rt[:, best, :, 0:1], rt[:, logit], AX.X, ALU.max))
                both(lambda t: dve.scalar_tensor_tensor(rt[:, hit, t], rt[:, logit, t],
                                                        rt[:, best, t, 0:1], desc_e[:],
                                                        ALU.is_equal, ALU.mult))
                own(dve.tensor_reduce(rt[:, best, :, 1:2], rt[:, hit], AX.X, ALU.max))
                both(lambda t: dve.tensor_scalar(rt[:, pick, t], desc_e[:], rt[:, best, t, 1:2],
                                                 None, ALU.is_equal))
            dve.tensor_tensor(rt[:, 4], rt[:, 3], rt[:, 8], ALU.add).then_inc(chosen, 1)
            dve.tensor_tensor(rt[:, 9, :, 0:1], rt[:, 6, :, 0:1], rt[:, 1, :, 0:1], ALU.subtract
                              ).then_inc(rexp_in, 1)
            dve.wait_ge(rexp, 1)
            own(dve.tensor_scalar(rt[:, 11, :, 0:1], rt[:, 10, :, 0:1], 1.0, None, ALU.add))
            own(dve.reciprocal(rt[:, 11, :, 0:1], rt[:, 11, :, 0:1]))
            own(dve.tensor_tensor(rt[:, 11, :, 1:2], rt[:, 11, :, 0:1], rt[:, 10, :, 0:1], ALU.mult))
            for t in range(TT):
                own(dve.tensor_scalar(rt[:, 12, t], rt[:, 3, t], rt[:, 11, t, 0:1], None, ALU.mult))
                own(dve.scalar_tensor_tensor(job_w[:, t, 0:E], rt[:, 8, t], rt[:, 11, t, 1:2],
                                             rt[:, 12, t], ALU.mult, ALU.add))
            dve.wait_ge(count_ps, 1)
            dve.wait_ge(chosen, 1)
            pos = ps[:, 5, 0:16].rearrange("p (t e) -> p t e", t=TT)
            own(dve.tensor_scalar(rt[:, 13], pos, 1.0, None, ALU.add))
            own(dve.tensor_tensor(rt[:, 13], rt[:, 13], rt[:, 4], ALU.mult))
            own(dve.tensor_scalar(job_pos[:, :, 0:E], rt[:, 13], -1.0, None, ALU.add))
            own(dve.tensor_scalar(ovf[:, 0], ps[:, 5, 16:24], float(P), None, ALU.is_gt))
            dve.memset(ssq[:], 0.0).then_inc(job_done, 1)

            n = MOE_BASE

            def one_hot(o):
                if loop.reg is not None:
                    dve.wait_ge(scatT_ps, loop.at("job", o))
                for t in range(TT):
                    at = job_pos[:, t, bass.ds(loop.reg + o, 1)] if loop.reg is not None \
                        else job_pos[:, t, 0:1]
                    dve.tensor_scalar(slots[:, t, :], iota[:], at, None, ALU.is_equal
                                      ).then_inc(slots_ready, 1)

            def gathered(o):
                for half in range(2):
                    dve.wait_ge(xg_hi_ready, loop.at("half", 2 * o + half + 1))
                    c = slice(4 * half, 4 * half + 4)
                    dve.tensor_tensor(xT_lo[:, c, 0:P],
                                      ps[:, 2 + half, :].rearrange("p (c t) -> p c t", t=P),
                                      xT_hi[:, c, 0:P].bitcast(F32), ALU.subtract
                                      ).then_inc(xg_ready, 1)

            def hid_low(f):
                dve.wait_ge(e_hid_hi, loop.at("block", f + 1))
                dve.tensor_tensor(hid_lo[:, f % 2, 0:512], ps[:, 4 + f % 2, :],
                                  hid_hi[:, f % 2, 0:512].bitcast(F32), ALU.subtract
                                  ).then_inc(e_hid, 1)

            def e_product(f, o=0):
                dve.wait_ge(e_sil, loop.at("block", f + 1 + EB * o))
                dve.tensor_tensor(prod[:, 0:512], silu[:, 0:512], ps[:, 2 * (f % 2) + 1, :],
                                  ALU.mult).then_inc(e_prod, 1)

            def add_job():
                dve.wait_ge(job_done, loop.at("job", 1))
                for t in range(TT):
                    dve.wait_ge(scat_ps, loop.at("tile", t + 1))
                    ht = h[:, t, :].rearrange("p (b c) -> p b c", b=2)
                    w = job_w[:, t, bass.ds(loop.reg, 1)]
                    ins = dve.scalar_tensor_tensor(ht, ps[:, 2:4, :] if t == 0 else ps[:, 4:6, :],
                                                   w, ht, ALU.mult, ALU.add)
                    ins.then_inc((tile0_done, job_done)[t], 1)

            def extra_table():
                own(dve.tensor_tensor_scan(ovf[:, 1], ones[:, 0:E], ovf[:, 0], 0.0, ALU.mult, ALU.add))
                own(dve.tensor_scalar(table[:, 3:4], ovf[:, 1, E - 1:E], float(E), None, ALU.add))

            def extra_row(r):
                own(dve.scalar_tensor_tensor(ovf[:, 2], ovf[:, 1], float(r + 1), ovf[:, 0],
                                             ALU.is_equal, ALU.mult))
                own(dve.tensor_tensor(ovf[:, 3], ovf[:, 2], iota_e[:], ALU.mult))
                own(dve.tensor_reduce(table[:, r:r + 1], ovf[:, 3], AX.X, ALU.add))
                for t in range(TT):
                    own(dve.scalar_tensor_tensor(ovf[:, 4], job_pos[:, t, 0:E], -float(P), ovf[:, 2],
                                                 ALU.add, ALU.mult))
                    own(dve.tensor_reduce(job_pos[:, t, E + r:E + r + 1], ovf[:, 4], AX.X, ALU.add))
                    own(dve.tensor_tensor(ovf[:, 5], job_w[:, t, 0:E], ovf[:, 2], ALU.mult))
                    own(dve.tensor_reduce(job_w[:, t, E + r:E + r + 1], ovf[:, 5], AX.X, ALU.add))

            def table_done():
                dve.tensor_copy(table_i[:], table[0:1, :]).then_inc(table_ready, 1)

            def rest_of_job(then_next, with_table=False):
                for i in range(4, JOB_PIECES + (4 if then_next else 0)):
                    if i == JOB_PIECES - 4:
                        hid_low(EB - 1)
                    for f in range(1, EB):
                        if i == gate_piece(f, 1) + 2:
                            dve.wait_ge(piece_used, loop.at("piece", n + i + 1))
                            e_product(f)
                    if then_next or i + NSPLIT < JOB_PIECES:
                        split(n + i + NSPLIT)
                    for f in range(1, EB):
                        if i == gate_piece(f, 1):
                            hid_low(f - 1)
                    if i == JOB_PIECES // 2 and then_next:
                        one_hot(1)
                    if with_table:
                        if i == 6:
                            extra_table()
                        if i in (10, 14, 18):
                            extra_row((i - 10) // 4)
                        if i == 20:
                            table_done()
                    if i == JOB_PIECES - 3 and then_next:
                        gathered(1)
                    if i == JOB_PIECES - 1:
                        for c in range(2):
                            dve.wait_ge(o_hi_ready, loop.at("half", c + 1))
                            dve.tensor_tensor(o_lo[:, c, :], ps[:, 6 + c, :],
                                              o_hi[:, c, :].bitcast(F32), ALU.subtract
                                              ).then_inc(o_ready, 1)
                        if not then_next:
                            add_job()
                    if i == JOB_PIECES + 1:
                        add_job()
                    if i == JOB_PIECES + 3:
                        e_product(0, 1)

            def start_of_job():
                gathered(0)
                for i in range(4):
                    split(n + i + NSPLIT)
                e_product(0)

            one_hot(0)
            start_of_job()
            with dve.Fori(0, E - 1) as j:
                loop.reg, loop.per = j, PER_JOB
                rest_of_job(then_next=True)
            loop.reg = E - 1
            rest_of_job(then_next=False, with_table=True)
            dve.wait_ge(table_ready, 1)
            jobs = dve.value_load(table_i[0:1, 3:4], min_val=E, max_val=JOBS)
            with dve.Fori(E, JOBS) as j:
                with dve.If(j < jobs):
                    loop.reg = j
                    one_hot(0)
                    for i in range(NSPLIT):
                        split(n + i)
                    start_of_job()
                    rest_of_job(then_next=False)
            loop.reg = None
            norm_rows(4, 6)

        @block.tensor
        def _(pe):
            loop = Loop()

            def passes(acc, x_hi, x_lo, w_hi, w_lo, start, stop, weights_move):
                for m, (a, b) in enumerate(((x_hi, w_hi), (x_lo, w_hi), (x_hi, w_lo))):
                    lhs, rhs = (a, b) if weights_move else (b, a)
                    ins = pe.matmul(acc, lhs, rhs, start=start and m == 0, stop=stop and m == 2,
                                    skip_group_check=True)
                return ins

            def piece(i, k):
                pe.wait_ge(lo_ready, loop.at("piece", i + 1))
                return (whi[:, i % NSPLIT, :].rearrange("p (k n) -> p k n", k=k),
                        wlo[:, i % NSPLIT, :].rearrange("p (k n) -> p k n", k=k))

            def transpose_half(tiles, half, bank, norm=None):
                for t in range(TT):
                    if norm is not None and half == 0:
                        pe.wait_ge(y_first, TT * norm + t + 1)
                    else:
                        pe.wait_ge(y_ready, tiles + t + 1)
                    for c in range(4):
                        c0 = 512 * half + c * P
                        ins = pe.transpose(ps[:, bank + t, c * P:(c + 1) * P], y[:, t, c0:c0 + P],
                                           ident[:])
                    ins.then_inc(xT_ps, 1)

            def transpose_rows(tiles, norm):
                for half in range(2):
                    transpose_half(tiles, half, 2 * half, norm)

            def columns_out(i, half, bank):
                hi, lo = piece(i, 4)
                for c in range(4):
                    acc = ps[:, bank + c // 2, 256 * (c % 2):256 * (c % 2) + 256]
                    for k in range(4):
                        kk = 4 * half + k
                        ins = passes(acc, xT_hi[:, kk, :], xT_lo[:, kk, :],
                                     hi[:, k, c * P:(c + 1) * P], lo[:, k, c * P:(c + 1) * P],
                                     start=half == 0 and k == 0 and c % 2 == 0,
                                     stop=half == 1 and k == 3, weights_move=False)
                ins.then_inc(piece_used, 1)

            def tokens_out(i, half, bank):
                hi, lo = piece(i, 4)
                for t in range(TT):
                    s = slice(t * P, (t + 1) * P)
                    for k in range(4):
                        kk = 4 * half + k
                        ins = passes(ps[:, bank + t, :], xT_hi[:, kk, s], xT_lo[:, kk, s],
                                     hi[:, k, :], lo[:, k, :], start=half == 0 and k == 0,
                                     stop=half == 1 and k == 3, weights_move=True)
                ins.then_inc(piece_used, 1)

            def two_rows_out(i, hi_of, lo_of, first, last, chunks=(0, 1)):
                hi, lo = piece(i, 2)
                for t in range(TT):
                    for c in range(2):
                        s = slice(c * 512, (c + 1) * 512)
                        for kk in chunks:
                            ins = passes(ps[:, 4 + 2 * t + c, :], hi_of(kk, t), lo_of(kk, t),
                                         hi[:, kk, s], lo[:, kk, s], start=first and kk == 0,
                                         stop=last and kk == 1, weights_move=True)
                        if last and (t, c) != (1, 1):
                            ins.then_inc(sums_out, 1)
                if 1 in chunks:
                    ins.then_inc(piece_used, 1)

            def mixer(l):
                n, q = MIX_BASE[l], X_MIX[l]
                transpose_rows(Y_MIX[l], 2 * l)

                def gates():
                    pe.wait_ge(wif_ready, 1)
                    for g in range(2):
                        for k in range(KC):
                            w = slice(8 * k + 4 * g, 8 * k + 4 * g + 4)
                            ins = passes(ps[0:HM, 7, 256 * g:256 * g + 256], xT_hi[:, k, :],
                                         xT_lo[:, k, :], wif_hi[:, l, w], wif_lo[:, l, w],
                                         start=k == 0, stop=k == KC - 1, weights_move=False)
                    ins.then_inc(grow_ps, 1)

                def conv_parameters():
                    pe.wait_ge(small_in, SMALL)
                    for c in range(KC):
                        ins = pe.transpose(ps[:, 6, 128 + 10 * c:138 + 10 * c],
                                           convrow[:, c * P:(c + 1) * P], ident[0:10, 0:10])
                    ins.then_inc(conv_ps, 1)

                def gate_columns():
                    pe.wait_ge(grows, l + 1)
                    for m, r in ((0, 6), (1, 5)):
                        for t in range(TT):
                            c = 64 + 8 * m + 4 * t
                            ins = pe.transpose(ps[:, 6, c:c + HM], rows[r][:, t * P:(t + 1) * P],
                                               ident[0:HM, 0:HM])
                    ins.then_inc(gcol_ps, 1)

                def head_scores(hd):
                    k = 4 * l + hd
                    if hd == 0:
                        pe.wait_ge(silu_done, 2 * (l + 1))
                        pe.wait_ge(gcol, 2 * (l + 1))
                        pe.wait_ge(proj_out, 7 * l + VM + 1)
                    else:
                        pe.wait_ge(decay_ready, 2 * k)
                    pe.matmul(ps[:, 2, 0:256], sel[:, hd, :], rows[7], start=True, stop=False,
                              skip_group_check=True)
                    pe.matmul(ps[:, 2, 256:384], sel[:, hd, :], rows[7][:, P:], start=False,
                              stop=False, skip_group_check=True)
                    pe.matmul(ps[:, 2, 0:P], ident_b[:], mask_m[:], start=False, stop=True,
                              skip_group_check=True)
                    pe.matmul(ps[:, 2, 256:384], ident_b[:], mask_m[:], start=False, stop=True,
                              skip_group_check=True).then_inc(head_ps, 1)
                    if hd:
                        pe.wait_ge(pT_ready, k)
                    pe.matmul(ps[:, 3, 0:256], qkc[:, 4 + hd, 0:P], qkc[:, hd, :], start=True,
                              stop=True, skip_group_check=True)
                    pe.matmul(ps[:, 3, 256:384], qkc[:, 4 + hd, P:], qkc[:, hd, P:], start=True,
                              stop=True, skip_group_check=True).then_inc(head_ps, 1)

                def head_values(hd):
                    k = 4 * l + hd
                    pe.wait_ge(pT_ready, k + 1)
                    if hd < 2:
                        pe.wait_ge(proj_out, 7 * (l + 1))
                    else:
                        pe.wait_ge(num_out, 4 * (k - 1))
                    w = DHM + 1
                    acc = ps[:, hd % 2, :]
                    pe.matmul(acc[:, 0:w], pT[:, hd % 2, 0:P], vm[:, 0, hd, 0:w], start=True,
                              stop=True, skip_group_check=True)
                    pe.matmul(acc[:, 130:130 + w], pT[:, hd % 2, P:2 * P], vm[:, 0, hd, 0:w],
                              start=True, stop=False, skip_group_check=True)
                    pe.matmul(acc[:, 130:130 + w], pT[:, hd % 2, 2 * P:], vm[:, 1, hd, 0:w],
                              start=False, stop=True, skip_group_check=True).then_inc(num_ps, 1)

                def pair_scores(p):
                    if p == 0:
                        pe.wait_ge(proj_out, 7 * l + KS + 1)
                    for a in range(2):
                        s = slice(64 * a, 64 * a + 64)
                        z = ps[:, 4 + a, :]
                        pe.matmul(z[:, 0:256], ksT[s, p, 0:P], qsT[s, p, :], start=True, stop=False,
                                  skip_group_check=True)
                        pe.matmul(z[:, 256:384], ksT[s, p, P:], qsT[s, p, P:], start=False,
                                  stop=False, skip_group_check=True)
                        for c in (0, 256):
                            ins = pe.matmul(z[:, c:c + P], ident_b[:], mask_s[:], start=False,
                                            stop=False, skip_group_check=True)
                    ins.then_inc(z_ps, 1)

                def pair_sums(p):
                    pe.wait_ge(softp_ready, 4 * l + p + 1)
                    for a in range(2):
                        z = ps[:, 4 + a, :]
                        pe.matmul(z[:, 0:256], tri_neg[:], softp[:, a, 0:256], start=False, stop=False,
                                  skip_group_check=True)
                        pe.matmul(z[:, P:256], neg1[:], softp[:, a, 256:384], start=False, stop=True,
                                  skip_group_check=True)
                        ins = pe.matmul(z[:, 256:384], tri_neg[:], softp[:, a, 256:384], start=False,
                                        stop=True, skip_group_check=True)
                    ins.then_inc(sum_ps, 1)

                def pair_values(p):
                    pe.wait_ge(aT_ready, 4 * l + p + 1)
                    if p == 0:
                        pe.wait_ge(proj_out, 7 * l + VS + 1)
                    else:
                        pe.wait_ge(av_out, 4 * l + p)
                    for a in range(2):
                        s = slice(64 * (2 * p + a), 64 * (2 * p + a) + 64)
                        o0, o1 = slice(64 * a, 64 * a + 64), slice(P + 64 * a, P + 64 * a + 64)
                        pe.matmul(ps[:, 7, o0], aT[:, a, 0:P], vs[:, 0, s], start=True, stop=True,
                                  skip_group_check=True)
                        pe.matmul(ps[:, 7, o1], aT[:, a, P:256], vs[:, 0, s], start=True, stop=False,
                                  skip_group_check=True)
                        ins = pe.matmul(ps[:, 7, o1], aT[:, a, 256:384], vs[:, 1, s], start=False,
                                        stop=True, skip_group_check=True)
                    ins.then_inc(av_ps, 1)

                for b in range(BLOCKS):
                    if b >= 2:
                        pe.wait_ge(proj_out, 7 * l + b - 1)
                    for half in range(2):
                        i = 2 * b + half
                        out_of = tokens_out if b in (VS, VM, OM) else columns_out
                        if b == 0:
                            pe.wait_ge(xT_ready, 2 * (q + half) + 2)
                        out_of(n + i, half, 2 * (b % 2))
                        if i == 1:
                            gates()
                        if i == 1 and l == 0:
                            conv_parameters()
                        if i == 4:
                            gate_columns()
                        if i % 2 == 0 and 6 <= i <= 12:
                            pair_values(i // 2 - 3)
                        if i % 2 == 0 and 4 <= i <= 10:
                            pair_scores(i // 2 - 2)
                        if i % 2 == 1 and 5 <= i <= 11:
                            pair_sums(i // 2 - 2)
                        if i == 12:
                            head_scores(0)
                head_scores(1)
                head_values(0)

                def out_rows(i, chunks=(0, 1)):
                    c0 = 2 * OUT_PIECES[i]
                    two_rows_out(n + 2 * BLOCKS + i,
                                 lambda kk, t: xT_hi[:, c0 + kk, t * P:(t + 1) * P],
                                 lambda kk, t: xT_lo[:, c0 + kk, t * P:(t + 1) * P],
                                 first=i == 0, last=i == 3, chunks=chunks)

                transpose_half(Y_MIX[l] + 2, 1, 4)
                head_scores(2)
                head_values(1)
                pe.wait_ge(xT_ready, 2 * (q + 2) + 2)
                out_rows(0, (0,))
                head_scores(3)
                head_values(2)
                head_values(3)
                out_rows(0, (1,))
                out_rows(1, (0,))
                transpose_half(Y_MIX[l] + 4, 0, 0)
                out_rows(1, (1,))
                pe.wait_ge(xT_ready, 2 * (q + 3) + 2)
                out_rows(2)
                out_rows(3)

            pe.wait_ge(consts, CONSTS)
            mixer(0)

            transpose_rows(Y_FFN, 1)
            n = FFN_BASE

            def gate_up(f):
                i = n + gate_piece(f, 0)
                if f:
                    pe.wait_ge(sil_ready, loop.at("block", f))
                for half in range(2):
                    if f == 0:
                        pe.wait_ge(xT_ready, 2 * (X_FFN + half) + 2)
                    columns_out(i + half, half, 0)
                if f:
                    pe.wait_ge(prod_ready, loop.at("block", f))
                for half in range(2):
                    columns_out(i + 2 + half, half, 2)

            def down(i, f):
                pe.wait_ge(hid_ready, loop.at("block", f + 1))
                for half in range(2):
                    def part(v):
                        hv = v[:, f % 2, :].rearrange("p (k t) -> p k t", k=4)
                        return lambda kk, t: hv[:, 2 * half + kk, t * P:(t + 1) * P]
                    two_rows_out(i + half, part(hid_hi), part(hid_lo), first=False, last=False)

            gate_up(0)
            for b in range(4, 8):
                for c in range(4):
                    pe.matmul(ps[:, b, c * P:(c + 1) * P], zero_b[:], zero_b[:], start=c == 0,
                              stop=False, skip_group_check=True)
            with pe.Fori(0, (DENSE_FULL - 1) // 2) as r:
                loop.reg, loop.per = r, {"piece": 12, "block": 2}
                for f in (1, 2):
                    gate_up(f)
                    down(n + 8 + 6 * (f - 1), f - 1)
            loop.reg = None
            n += 6 * DENSE_FULL - 2
            for m in range(2):
                pe.wait_ge((sil_ready, prod_ready)[m], DENSE_FULL)
                pe.wait_ge(lo_ready, n + 1)
                hi = whi[:, n % NSPLIT, 0:KC * TAIL].rearrange("p (k n) -> p k n", k=KC)
                lo = wlo[:, n % NSPLIT, 0:KC * TAIL].rearrange("p (k n) -> p k n", k=KC)
                for c in range(2):
                    s = slice(64 * c, 64 * c + P)
                    for k in range(KC):
                        ins = passes(ps[:, 2 * m, 256 * c:256 * c + 256], xT_hi[:, k, :],
                                     xT_lo[:, k, :], hi[:, k, s], lo[:, k, s], start=k == 0,
                                     stop=k == KC - 1, weights_move=False)
                ins.then_inc(piece_used, 1)
                n += 1
            down(n, DENSE_FULL - 1)
            n += 2
            pe.wait_ge(hid_ready, DENSE_FULL + 1)
            hi, lo = piece(n, 2)
            hv = [v[:, DENSE_FULL % 2, 0:512].rearrange("p (k t) -> p k t", k=2)
                  for v in (hid_hi, hid_lo)]
            for t in range(TT):
                ts = slice(t * P, (t + 1) * P)
                for c in range(2):
                    s = slice(c * 512, (c + 1) * 512)
                    for kk, k0 in ((0, 0), (1, 64)):
                        ins = passes(ps[:, 4 + 2 * t + c, :], hv[0][k0:, kk, ts], hv[1][k0:, kk, ts],
                                     hi[k0:, kk, s], lo[k0:, kk, s], start=False, stop=kk == 1,
                                     weights_move=True)
                    if (t, c) != (1, 1):
                        ins.then_inc(sums_out, 1)
            ins.then_inc(piece_used, 1)
            mixer(1)

            transpose_rows(Y_ROUTE, 3)
            for half in range(2):
                for t in range(TT):
                    pe.wait_ge(xT_hi_ready, 2 * (X_ROUTE + half) + t + 1)
                    for k in range(4 * half, 4 * half + 4):
                        ins = pe.matmul(ps[:, 4 + 2 * t, 0:E], xT_f[:, k, t * P:(t + 1) * P],
                                        wr[:, k, :], start=k == 0, stop=k == KC - 1,
                                        skip_group_check=True)
            ins.then_inc(route_ps, 1)
            pe.wait_ge(chosen, 1)
            ch = rt[:, 4]
            pe.matmul(ps[:, 5, 0:8], tri[:], ch[:, 0], start=True, stop=True, skip_group_check=True)
            pe.matmul(ps[:, 5, 8:16], ones[:, 0:P], ch[:, 0], start=True, stop=False,
                      skip_group_check=True)
            pe.matmul(ps[:, 5, 8:16], tri[:], ch[:, 1], start=False, stop=True, skip_group_check=True)
            for t in range(TT):
                ins = pe.matmul(ps[:, 5, 16:24], ones[:, 0:P], ch[:, t], start=t == 0, stop=t == 1,
                                skip_group_check=True)
            ins.then_inc(count_ps, 1)

            n = MOE_BASE

            def gather(o):
                pe.wait_ge(slots_ready, loop.at("tile", TT * (1 + o)))
                for c in range(KC):
                    for t in range(TT):
                        ins = pe.matmul(ps[:, 2 + c // 4, P * (c % 4):P * (c % 4) + P],
                                        y[:, t, c * P:(c + 1) * P], slots[:, t, :],
                                        start=t == 0, stop=t == 1, skip_group_check=True)
                    if c % 4 == 3:
                        ins.then_inc(xg_ps, 1)

            def scatter_matrix():
                for t in range(TT):
                    ins = pe.transpose(ps[:, 6, t * P:(t + 1) * P], slots[:, t, :], ident[:])
                ins.then_inc(scatT_ps, 1)

            def product(i, bank, gathering=None):
                for half in range(2):
                    if gathering is not None:
                        pe.wait_ge(xg_ready, loop.at("half", 2 * gathering + half + 1))
                    hi, lo = piece(n + i + half, 4)
                    for k in range(4):
                        kk = 4 * half + k
                        ins = passes(ps[:, bank, :], xT_hi[:, kk, 0:P], xT_lo[:, kk, 0:P],
                                     hi[:, k, :], lo[:, k, :], start=half == 0 and k == 0,
                                     stop=half == 1 and k == 3, weights_move=True)
                    ins.then_inc(piece_used, 1)

            def hid_transpose(f):
                pe.wait_ge(e_prod, loop.at("block", f + 1))
                if f >= 2:
                    pe.wait_ge(e_hid, loop.at("block", f - 1))
                for k in range(4):
                    ins = pe.transpose(ps[:, 4 + f % 2, k * P:(k + 1) * P],
                                       prod[:, k * P:(k + 1) * P], ident[:])
                ins.then_inc(e_hidT, 1)

            def down_piece_job(f, half):
                hi, lo = piece(n + down_piece(f, half, EB), 2)
                last = f == EB - 1 and half == 1
                order = [(kk, c) for kk in range(2) for c in range(2)]
                if last:
                    order = [(kk, c) for c in range(2) for kk in range(2)]
                for kk, c in order:
                    hs = slice((2 * half + kk) * P, (2 * half + kk + 1) * P)
                    s = slice(c * 512, (c + 1) * 512)
                    ins = passes(ps[:, 6 + c, :], hid_hi[:, f % 2, hs], hid_lo[:, f % 2, hs],
                                 hi[:, kk, s], lo[:, kk, s],
                                 start=f == 0 and half == 0 and kk == 0,
                                 stop=last and kk == 1, weights_move=True)
                    if last and (kk, c) == (1, 0):
                        ins.then_inc(o_sum, 1)
                ins.then_inc(piece_used, 1)

            def down_job(f):
                pe.wait_ge(e_hid, loop.at("block", f + 1))
                down_piece_job(f, 0)
                if f == EB - 2:
                    hid_transpose(EB - 1)
                down_piece_job(f, 1)

            def scatter():
                for c in range(2):
                    pe.wait_ge(o_ready, loop.at("half", c + 1))
                    for t in range(TT):
                        bank = ps[:, 2 + 2 * t + c, :]
                        pe.matmul(bank, scatT[:, t, :], o_hi[:, c, :], start=True, stop=False,
                                  skip_group_check=True)
                        ins = pe.matmul(bank, scatT[:, t, :], o_lo[:, c, :], start=False,
                                        stop=True, skip_group_check=True)
                        if c == 1:
                            ins.then_inc(scat_ps, 1)

            def start_of_job():
                gather(0)
                scatter_matrix()
                product(0, 0, gathering=0)
                product(2, 1)

            def rest_of_job(then_next):
                for f in range(1, EB):
                    if f == 1:
                        pe.wait_ge(job_done, loop.at("job", 1))
                        pe.wait_ge(scatT_ready, loop.at("job", 1))
                    else:
                        pe.wait_ge(e_prod, loop.at("block", f - 1))
                    product(gate_piece(f, 0), 2 * (f % 2))
                    hid_transpose(f - 1)
                    product(gate_piece(f, 0) + 2, 2 * (f % 2) + 1)
                    down_job(f - 1)
                if then_next:
                    gather(1)
                down_job(EB - 1)
                if then_next:
                    product(JOB_PIECES, 0, gathering=1)
                scatter()
                if then_next:
                    scatter_matrix()
                    product(JOB_PIECES + 2, 1)

            start_of_job()
            with pe.Fori(0, E - 1) as j:
                loop.reg, loop.per = j, PER_JOB
                rest_of_job(then_next=True)
            loop.reg = E - 1
            rest_of_job(then_next=False)
            pe.wait_ge(table_ready, 1)
            jobs = pe.value_load(table_i[0:1, 3:4], min_val=E, max_val=JOBS)
            with pe.Fori(E, JOBS) as j:
                with pe.If(j < jobs):
                    loop.reg = j
                    pe.wait_ge(job_done, loop.at("job", 1))
                    start_of_job()
                    rest_of_job(then_next=False)


def arrival(i, loop):
    last = FFN_BASE + FFN_PIECES - 1
    more = 16 if i >= last and (i - last) % NRAW == 0 else 0
    n = 16 * (i // NRAW + 1) + more
    return n if loop.reg is None else loop.reg * (16 * (loop.per["piece"] // NRAW)) + n


_INS = ['x', 'norm_mix_g', 'w_in', 'b_igate', 'b_fgate', 'conv_w', 'conv_b', 'g_mlstm', 'g_sb',
        'w_out', 'norm_ffn_g', 'ffn_w_gate', 'ffn_w_up', 'ffn_w_down', 'w_router', 'moe_w_gate',
        'moe_w_up', 'moe_w_down', 'norm_final_g']


def kernel(**inputs):
    import numpy as np
    import concourse.bacc as bacc
    from concourse.bass_utils import run_bass_kernel_spmd

    nc = bacc.Bacc("TRN2", target_bir_lowering=False, num_devices=1)
    arrays, args = {}, []
    for name in _INS:
        a = np.ascontiguousarray(inputs[name])
        arrays[f"in_{name}_dram"] = a
        args.append(nc.dram_tensor(f"in_{name}_dram", a.shape, mybir.dt.from_np(a.dtype),
                                   kind="ExternalInput").ap())
    args.append(nc.dram_tensor("out_dram", (1, TT * P, D), F32, kind="ExternalOutput").ap())
    trunk(nc, *args)
    r = run_bass_kernel_spmd(nc, [arrays], core_ids=[0])
    return r.results[0]["out_dram"]
```
